# Optimizing a Trainium2 kernel written in Bass

```python
import math
import jax, jax.numpy as jnp
from jax import lax
import numpy as np

D_MODEL = 2048
BATCH = 1
SEQ = 256
DEPTH = 1

D_MIX = D_MODEL
CONV_CH = D_MIX // 2
CONV_GROUPS = 8
CONV_WIDTH = 31
N_HEADS = 8
QK_NOPE_DIM = 128
QK_ROPE_DIM = 64
QK_DIM = QK_NOPE_DIM + QK_ROPE_DIM
V_DIM = 128
Q_RANK = 512
KV_RANK = 256
D_IN_PROJ = 2 * CONV_CH + Q_RANK + KV_RANK + QK_ROPE_DIM
D_FF = 5504
ROPE_THETA = 10000.0
Q_BLOCK = 128
EPS = 1e-6

kernel_name = "hybrid_conformer_mla_parallel_layer"

def rms_norm(x, g):
    xf = x.astype(jnp.float32)
    y = xf * lax.rsqrt(jnp.mean(xf * xf, axis=-1, keepdims=True) + EPS)
    return (y * g.astype(jnp.float32)).astype(x.dtype)

def swiglu(x, w_gate, w_up, w_down):
    return (jax.nn.silu(x @ w_gate) * (x @ w_up)) @ w_down

def rope(x, positions):
    r = x.shape[-1]
    half = r // 2
    inv_freq = ROPE_THETA ** (-(jnp.arange(half, dtype=jnp.float32) * 2.0 / r))
    ang = positions.astype(jnp.float32)[..., None] * inv_freq
    cos = jnp.cos(ang)[:, :, None, :]
    sin = jnp.sin(ang)[:, :, None, :]
    xf = x.astype(jnp.float32)
    x1, x2 = xf[..., :half], xf[..., half:]
    out = jnp.concatenate([x1 * cos - x2 * sin, x2 * cos + x1 * sin], axis=-1)
    return out.astype(x.dtype)

def block_attention(q, k, v):
    b, s, h, d = q.shape
    nblk = s // Q_BLOCK
    scale = 1.0 / math.sqrt(d)
    qb = q.reshape(b, nblk, Q_BLOCK, h, d).transpose(1, 0, 2, 3, 4)

    def one_block(qi):
        sc = jnp.einsum('bqhd,bkhd->bhqk', qi, k).astype(jnp.float32) * scale
        p = jax.nn.softmax(sc, axis=-1).astype(v.dtype)
        return jnp.einsum('bhqk,bkhd->bqhd', p, v)

    o = lax.map(one_block, qb)
    return o.transpose(1, 0, 2, 3, 4).reshape(b, s, h, v.shape[-1])

def conv_module(z_conv, dw_kernel, dw_bias, conv_norm):
    u = z_conv[..., :CONV_CH] * jax.nn.sigmoid(z_conv[..., CONV_CH:])
    pad = CONV_WIDTH // 2
    y = lax.conv_general_dilated(
        u, dw_kernel.astype(u.dtype)[:, None, :],
        window_strides=(1,), padding=[(pad, pad)],
        dimension_numbers=('NWC', 'WIO', 'NWC'),
        feature_group_count=CONV_CH)
    y = y + dw_bias
    return jax.nn.silu(rms_norm(y, conv_norm))

def mla(z_q, z_kv, z_kpe, positions, q_norm, w_uq, kv_norm, w_ukv, q_head_norm, k_head_norm):
    b, s = z_q.shape[0], z_q.shape[1]
    q = (rms_norm(z_q, q_norm) @ w_uq).reshape(b, s, N_HEADS, QK_DIM)
    kv = (rms_norm(z_kv, kv_norm) @ w_ukv).reshape(b, s, N_HEADS, QK_NOPE_DIM + V_DIM)
    k_nope, v = kv[..., :QK_NOPE_DIM], kv[..., QK_NOPE_DIM:]
    k_pe = jnp.broadcast_to(z_kpe[:, :, None, :], (b, s, N_HEADS, QK_ROPE_DIM))
    k = jnp.concatenate([k_nope, k_pe], axis=-1)
    q = rms_norm(q, q_head_norm)
    k = rms_norm(k, k_head_norm)
    q = jnp.concatenate([q[..., :QK_NOPE_DIM], rope(q[..., QK_NOPE_DIM:], positions)], axis=-1)
    k = jnp.concatenate([k[..., :QK_NOPE_DIM], rope(k[..., QK_NOPE_DIM:], positions)], axis=-1)
    o = block_attention(q, k, v)
    return o.reshape(b, s, N_HEADS * V_DIM)

def setup_inputs(seed: int = 0) -> dict:
    key = jax.random.key(seed)
    ks = jax.random.split(key, 24)
    f32 = jnp.float32

    def w(k, shape, fan_in):
        return jax.random.normal(k, shape, f32) * (fan_in ** -0.5)

    def gain(k, shape):
        return 1.0 + 0.02 * jax.random.normal(k, shape, f32)

    L = DEPTH
    x = jax.random.normal(ks[0], (BATCH, SEQ, D_MODEL), f32)
    positions = jnp.broadcast_to(jnp.arange(SEQ, dtype=jnp.int32)[None, :], (BATCH, SEQ))
    return {
        "x": x,
        "positions": positions,
        "ffn1_norm": gain(ks[1], (L, D_MODEL)),
        "ffn1_w_gate": w(ks[2], (L, D_MODEL, D_FF), D_MODEL),
        "ffn1_w_up": w(ks[3], (L, D_MODEL, D_FF), D_MODEL),
        "ffn1_w_down": w(ks[4], (L, D_FF, D_MODEL), D_FF),
        "mix_norm": gain(ks[5], (L, D_MODEL)),
        "w_in": w(ks[6], (L, D_MODEL, D_IN_PROJ), D_MODEL),
        "q_norm": gain(ks[7], (L, Q_RANK)),
        "w_uq": w(ks[8], (L, Q_RANK, N_HEADS * QK_DIM), Q_RANK),
        "kv_norm": gain(ks[9], (L, KV_RANK)),
        "w_ukv": w(ks[10], (L, KV_RANK, N_HEADS * (QK_NOPE_DIM + V_DIM)), KV_RANK),
        "q_head_norm": gain(ks[11], (L, QK_DIM)),
        "k_head_norm": gain(ks[12], (L, QK_DIM)),
        "dw_kernel": w(ks[13], (L, CONV_WIDTH, CONV_CH), CONV_WIDTH),
        "dw_bias": 0.02 * jax.random.normal(ks[14], (L, CONV_CH), f32),
        "conv_norm": gain(ks[15], (L, CONV_CH)),
        "w_out": w(ks[16], (L, D_MIX, D_MODEL), D_MIX),
        "ffn2_norm": gain(ks[17], (L, D_MODEL)),
        "ffn2_w_gate": w(ks[18], (L, D_MODEL, D_FF), D_MODEL),
        "ffn2_w_up": w(ks[19], (L, D_MODEL, D_FF), D_MODEL),
        "ffn2_w_down": w(ks[20], (L, D_FF, D_MODEL), D_FF),
        "final_norm": gain(ks[21], (L, D_MODEL)),
    }

def reference(x, positions, ffn1_norm, ffn1_w_gate, ffn1_w_up, ffn1_w_down, mix_norm, w_in,
              q_norm, w_uq, kv_norm, w_ukv, q_head_norm, k_head_norm, dw_kernel, dw_bias,
              conv_norm, w_out, ffn2_norm, ffn2_w_gate, ffn2_w_up, ffn2_w_down, final_norm):
    c0 = 2 * CONV_CH
    c1 = c0 + Q_RANK
    c2 = c1 + KV_RANK
    for l in range(DEPTH):
        x = x + 0.5 * swiglu(rms_norm(x, ffn1_norm[l]), ffn1_w_gate[l], ffn1_w_up[l], ffn1_w_down[l])
        h = rms_norm(x, mix_norm[l])
        z = h @ w_in[l]
        a_out = conv_module(z[..., :c0], dw_kernel[l], dw_bias[l], conv_norm[l])
        b_out = mla(z[..., c0:c1], z[..., c1:c2], z[..., c2:], positions,
                    q_norm[l], w_uq[l], kv_norm[l], w_ukv[l], q_head_norm[l], k_head_norm[l])
        x = x + jnp.concatenate([a_out, b_out], axis=-1) @ w_out[l]
        x = x + 0.5 * swiglu(rms_norm(x, ffn2_norm[l]), ffn2_w_gate[l], ffn2_w_up[l], ffn2_w_down[l])
        x = rms_norm(x, final_norm[l])
    return x


_drawn_inputs = setup_inputs


def setup_inputs(seed=0):
    import zlib

    import numpy as np

    out = dict(_drawn_inputs(seed))
    spreads = {}
    factors = {'ffn1_norm': 6.285,
     'mix_norm': 6.082,
     'q_norm': 8.0,
     'kv_norm': 8.0,
     'q_head_norm': 8.0,
     'k_head_norm': 8.0,
     'dw_bias': 3.903,
     'conv_norm': 6.136,
     'ffn2_norm': 7.687,
     'final_norm': 2.766}
    for name, (base, spread) in spreads.items():
        noise = np.random.default_rng([zlib.crc32(name.encode()), seed]).standard_normal(out[name].shape)
        drawn = base * np.exp(spread * noise) if base else spread * noise
        out[name] = __import__('jax').numpy.asarray(drawn.astype(out[name].dtype))
    for name, factor in factors.items():
        out[name] = (out[name] * factor).astype(out[name].dtype)
    return out
```

```python
import concourse.bass as bass
import concourse.mybir as mybir
import numpy as np
from concourse.alu_op_type import AluOpType as ALU
from contextlib import ExitStack

F32, F32R, I32 = mybir.dt.float32, mybir.dt.float32r, mybir.dt.int32
ACT = mybir.ActivationFunctionType
AX = mybir.AxisListType
ds = bass.ds

P = 128
TOK = 256
TB = TOK // P
DM = 2048
DT = DM // P
FF = 5504
CONV = 1024
CT = CONV // P
TAPS = 31
PAD = TAPS // 2
HEADS, NOPE, ROPE, VD = 8, 128, 64, 128
QK = NOPE + ROPE
QR, KVR = 512, 256
EPS = 1e-6
SCALE = QK ** -0.5
KC = 4
UNIT = 2048
PARTS = [(0, 16), (16, 16), (32, 11)]
TWO_PI = 2 * np.pi
MAGIC = 1.5 * 2.0 ** 23


def pi_chunks():
    left, out = TWO_PI, []
    for grid in (2.0 ** -9, 2.0 ** -21, 2.0 ** -33, 2.0 ** -45):
        c = np.floor(left / grid) * grid
        out.append(float(c))
        left -= c
    return out


GAIN_ROWS = [("ffn1_norm", 16), ("mix_norm", 16), ("ffn2_norm", 16), ("final_norm", 16), ("conv_norm", 8),
             ("dw_bias", 8), ("q_norm", 4), ("kv_norm", 2)]
GAIN_AT, _r = {}, 0
for _n, _c in GAIN_ROWS:
    GAIN_AT[_n] = _r
    _r += _c
G_QN, G_KN, G_QR, G_KR = _r, _r + 1, _r + 2, _r + 3
GAINS = _r + 4

FULL_PAIRS = [n // 2 for _, n in PARTS]
PAIR_COUNT = [(n + 1) // 2 for _, n in PARTS]
DOWN_UNITS = [(n + KC - 1) // KC for _, n in PARTS]
PART_UNITS = [KC * PAIR_COUNT[i] + 4 * DOWN_UNITS[i] for i in range(3)]
PART_GROUPS = [PAIR_COUNT[i] + 4 for i in range(3)]
FFN_UNITS, FFN_GROUPS, FFN_PAIRS = sum(PART_UNITS), sum(PART_GROUPS), sum(PAIR_COUNT)
MIX_UNITS, MIX_GROUPS = 48, 17
GLU_PAIRS = CT // 2


def build_layer(nc, io):
    stack = ExitStack()
    with stack:
        def sb(name, shape, dt=F32):
            return stack.enter_context(nc.sbuf_tensor(name, shape, dt))

        def sem(name):
            return stack.enter_context(nc.semaphore(name))

        X = sb("X", [P, DT, TOK])
        XN = sb("XN", [P, DT, 2 * TOK], F32R)
        H = sb("H", [P, 18, 2 * TOK], F32R)
        RAW = sb("RAW", [P, 2, UNIT])
        WHI = sb("WHI", [P, 2, UNIT], F32R)
        WLO = sb("WLO", [P, 2, UNIT], F32R)
        TOKS = sb("TOKS", [P, TB, DM])
        LOSUM = sb("LOSUM", [P, 4, TOK])
        SUM = sb("SUM", [P, 4, TOK])
        GATE = sb("GATE", [P, 2, TOK])
        HID = sb("HID", [P, 2, TOK])
        RINV = sb("RINV", [P, TOK])
        RINV2 = sb("RINV2", [P, TOK])
        ROOT = sb("ROOT", [P, TOK])
        SQ = sb("SQ", [P, 2, TOK])
        SQT = sb("SQT", [P, 2, TOK])
        U = sb("U", [P, CT, TOK + 2 * PAD])
        Y = sb("Y", [P, CT, TOK])
        KN = sb("KN", [P, HEADS, TOK])
        V = sb("V", [P, TB, HEADS * VD])
        KROT = sb("KROT", [P, TOK])
        KPSQ = sb("KPSQ", [ROPE, TOK])
        COS = sb("COS", [P, TOK])
        SIN = sb("SIN", [P, TOK])
        TAPW = sb("TAPW", [P, CT * TAPS])
        GAIN = sb("GAIN", [P, GAINS])
        IDENT = sb("IDENT", [P, P])
        ONES = sb("ONES", [P, P])
        SEL = sb("SEL", [P, HEADS, HEADS])
        EPST = sb("EPST", [P, 1])
        FREQ = sb("FREQ", [P, 4])
        QKG = sb("QKG", [P, 1])
        QSTAT = sb("QSTAT", [P, 4, 2 * HEADS])
        QRMS = sb("QRMS", [P, 2, 2 * HEADS])
        SMALL = sb("SMALL", [P, 2, 4, TB])
        YSTAT = sb("YSTAT", [P, 2, TB])

        PS = stack.enter_context(nc.psum_tensor("PS", [P, 8, 512], F32))

        QN = TOKS[:, 0, :].rearrange("p (t n) -> p t n", t=8)
        QROT = TOKS[:, 1, 0:1024].rearrange("p (t n) -> p t n", t=4)
        SQB = TOKS[:, 1, 1024:2048].rearrange("p (t n) -> p t n", t=4)
        U_flat = U[:, :, :].rearrange("p t n -> p (t n)")
        KRH = U_flat[:, 0:1024].rearrange("p (t n) -> p t n", t=4)
        QS = U_flat[:, 1024:1536].rearrange("p (e n) -> p e n", e=2)
        VS = U_flat[:, 1536:2048].rearrange("p (e k n) -> p e k n", e=2, k=2)
        EXPAND = U_flat[0:HEADS, 1024:2048]
        QRS = [RINV, KROT]
        PB = LOSUM[:, :, :].rearrange("p (e b) n -> p e b n", e=2)
        PN = SUM[:, :, :].rearrange("p (e b) n -> p e b n", e=2)
        PT = [GATE, HID]
        YG = KN[:, 0:4, :]
        KG, KSW = GATE[:, 0, :], GATE[:, 1, :]
        KRINV = GATE[0:HEADS, 1, :]
        GROWS = SUM[0:GAINS, 0, 0:P]
        TAPR = V[0:TAPS, 0, :]
        HALVES = FREQ[:, 2:4]
        TAB = Y

        sem_raw = [sem("raw_loaded_0"), sem("raw_loaded_1")]
        names = """whi_ready wlo_ready units_used banks_free losum_ready scaled gate_ready hid_ready
            h_hi_ready h_lo_ready x_updated x_hi_ready x_lo_ready sq_term sq_added stat_done root_ready rinv_ready
            x_loaded_0 x_loaded_1 ident_loaded consts_loaded gains_loaded taps_loaded pos_loaded expand_loaded x_turned gains_turned
            gains_ready taps_turned taps_ready ones_ready rope_step sin_ready trig_ready pads_ready glu_scaled sig_ready
            u_ready conv_dve conv_pool kv_scaled kv_normed kv_hi kv_lo kpe_gained kpe_moved kpe_mixed krot_ready kpe_sq
            zq_scaled zq_normed zq_hi zq_lo hsq_ready hstat_done kroot_ready krinv_ready kbcast_done
            k_scaled qstat_copied qstat_sum qroot_ready qrinv_ready qscale_ready qkg_ready qrot_gained qrot_moved
            qrot_mixed qrot_ready q_static v_static qr_static qr_zeroed scores_done max_ready bias_ready exp_ready den_ready
            probs_ready probs_turned probsT_ready o_done o_hi_ready o_lo_ready y_scaled y_silu a_hi_ready
            a_lo_ready y_gained y_turned y_copied y_scaled_out stored""".split()
        S = {n: sem(n) for n in names}
        (whi_ready, wlo_ready, units_used, banks_free, losum_ready, scaled, gate_ready, hid_ready,
         h_hi_ready, h_lo_ready, x_updated, x_hi_ready, x_lo_ready, sq_term, sq_added, stat_done, root_ready,
         rinv_ready, x_loaded_0, x_loaded_1, ident_loaded, consts_loaded, gains_loaded, taps_loaded, pos_loaded, expand_loaded, x_turned,
         gains_turned, gains_ready, taps_turned, taps_ready, ones_ready, rope_step, sin_ready, trig_ready, pads_ready,
         glu_scaled, sig_ready, u_ready, conv_dve, conv_pool, kv_scaled, kv_normed, kv_hi, kv_lo, kpe_gained, kpe_moved,
         kpe_mixed, krot_ready, kpe_sq, zq_scaled, zq_normed, zq_hi, zq_lo, hsq_ready, hstat_done,
         kroot_ready, krinv_ready, kbcast_done, k_scaled, qstat_copied, qstat_sum, qroot_ready, qrinv_ready,
         qscale_ready, qkg_ready, qrot_gained, qrot_moved, qrot_mixed, qrot_ready, q_static, v_static, qr_static, qr_zeroed,
         scores_done, max_ready, bias_ready, exp_ready, den_ready, probs_ready, probs_turned, probsT_ready, o_done,
         o_hi_ready, o_lo_ready, y_scaled, y_silu, a_hi_ready, a_lo_ready, y_gained, y_turned, y_copied, y_scaled_out,
         stored) = (S[n] for n in names)

        MIX_N, MIX_G, MIX_X = FFN_UNITS, FFN_GROUPS, 4 + 12
        FFN_N, FFN_G, FFN_X = [0, MIX_N + MIX_UNITS], [0, MIX_G + MIX_GROUPS], [4, MIX_X + 4]
        WO_N, WO_G = MIX_N + 32, MIX_G + 13
        KV_G, ZQ_G, V_G, K_G, Q_G, R_G = (MIX_G + i for i in (4, 5, 6, 7, 9, 11))
        ST_FFN1, ST_MIX, ST_KV, ST_ZQ, ST_CONV, ST_FFN2, ST_OUT = range(7)
        SQ_STEPS = [8, 8, 1, 2, 4, 8, 8]
        SQ_END = [sum(SQ_STEPS[:i + 1]) for i in range(7)]
        STAT_BANK = [4 - 4 * (g % 2) for g in FFN_G]

        ROPE_STEPS = 41

        def part_start(f, p):
            return (FFN_N[f] + sum(PART_UNITS[:p]), FFN_G[f] + sum(PART_GROUPS[:p]),
                    f * FFN_PAIRS + sum(PAIR_COUNT[:p]), FFN_X[f] + 4 * p)

        def over(r, n):
            return r.unsqueeze(1).broadcast_to([r.shape[0], n, TOK])

        def f32(a):
            return a.bitcast(F32)

        def gain(name, t):
            return GAIN[:, GAIN_AT[name] + t:GAIN_AT[name] + t + 1]

        def loads_by(n, c, uq_units):
            return n * 16 + (32 - 16 * (c % 2) + 32 * uq_units)

        CONV_DVE, CONV_POOL = [0, 2, 4, 5, 6], [1, 3, 7]
        DVE_STEPS, POOL_STEPS = TAPS + 1, 2 * TAPS - 1
        CONV_DVE_END, CONV_POOL_END = DVE_STEPS * len(CONV_DVE), POOL_STEPS * len(CONV_POOL)

        def window_of(t, k):
            return U[:, t, k:k + TOK], TAPW[:, t * TAPS + k:t * TAPS + k + 1]

        block = stack.enter_context(nc.Block())

        @block.sync
        def _(sp):
            slot_free_at = sp.alloc_register("slot_free_at")

            def load(n, c, pieces):
                if not (isinstance(n, int) and n < 2):
                    free_at = n - 1
                    if not isinstance(n, int):
                        sp.reg_mov(slot_free_at, free_at)
                        free_at = slot_free_at
                        sp.wait_ge(wlo_ready, 1)
                    sp.wait_ge(wlo_ready, free_at)
                for dst, src in pieces:
                    sp.dma_start(dst, src).then_inc(sem_raw[c % 2], 16)

            def slot(c, kc, w):
                return RAW[:, c % 2, 0:kc * w].rearrange("p (k w) -> p k w", w=w)

            def load_two(n, c, k0, wa, ca, wb, cb, w):
                v = slot(c, KC, 2 * w)
                load(n, c, [(v[:, :, 0:w], wa[:, k0:k0 + KC, ds(ca, w)]),
                            (v[:, :, w:2 * w], wb[:, k0:k0 + KC, ds(cb, w)])])

            def load_one(n, c, k0, kc, wa, ca, w):
                v, h = slot(c, kc, w), kc // 2
                load(n, c, [(v[:, 0:h, :], wa[:, k0:k0 + h, ds(ca, w)]),
                            (v[:, h:kc, :], wa[:, k0 + h:k0 + kc, ds(ca, w)])])

            def rows(w):
                return w[0].rearrange("(k p) n -> p k n", p=P)

            def ffn(f):
                wg, wu, wd = (rows(io[f"ffn{f + 1}_w_{s}"]) for s in ("gate", "up", "down"))
                for p, (t0, nt) in enumerate(PARTS):
                    n, du = part_start(f, p)[0], DOWN_UNITS[p]

                    def pair(q, at, w=2 * P):
                        for c in range(KC):
                            col = q * (2 * P) + t0 * P
                            load_two(at + c, c, KC * c, wg, col, wu, col, w)

                    pair(0, n)
                    pair(1, n + KC)
                    with sp.Fori(1, FULL_PAIRS[p] // 2) as i:
                        for e in range(2):
                            pair(i * 2 + e, i * (2 * KC) + (n + e * KC))
                    for q in range(FULL_PAIRS[p] // 2 * 2, PAIR_COUNT[p]):
                        pair(q, n + KC * q, P * min(2, nt - 2 * q))
                    n += KC * PAIR_COUNT[p]
                    with sp.Fori(0, 2) as i:
                        for e in range(2):
                            for u in range(du):
                                c = e * du + u
                                load_one(i * (2 * du) + (n + c), c, t0 + KC * u, min(KC, nt - KC * u),
                                         wd, i * (8 * P) + e * 4 * P, 4 * P)

            ffn(0)
            w_in, w_out = rows(io["w_in"]), rows(io["w_out"])
            w_kv = io["w_ukv"][0].rearrange("(k p) (h s d) -> p k s h d", p=P, s=2, d=P)
            w_q = io["w_uq"][0].rearrange("(k p) (h d) -> p k h d", p=P, d=QK)
            for j in range(GLU_PAIRS):
                for c in range(KC):
                    load_two(MIX_N + 4 * j + c, c, KC * c, w_in, 2 * j * P, w_in, CONV + 2 * j * P, 2 * P)
            for c in range(KC):
                load_one(MIX_N + 16 + c, c, KC * c, KC, w_in, 2 * CONV + QR, KVR + ROPE)
            for c in range(KC):
                load_one(MIX_N + 20 + c, c, KC * c, KC, w_in, 2 * CONV, QR)
            for n, s in ((24, 1), (26, 0)):
                for c in range(2):
                    v = RAW[:, c, 0:1024].rearrange("p (k h d) -> p k h d", k=2, d=P)
                    load(MIX_N + n + c, c, [(v[:, k], w_kv[:, k, s, 4 * c:4 * c + 4]) for k in range(2)])
            for n, d0, d in ((28, 0, NOPE), (30, NOPE, ROPE)):
                for c in range(2):
                    v = RAW[:, c, 0:KC * 4 * d].rearrange("p (k h d) -> p k h d", k=KC, d=d)
                    load(MIX_N + n + c, c, [(v[:, k], w_q[:, k, 4 * c:4 * c + 4, d0:d0 + d]) for k in range(KC)])
            with sp.Fori(0, 2) as i:
                for e in range(2):
                    for u, k0 in enumerate((8, 12, 0, 4)):
                        load_one(i * 8 + (WO_N + 4 * e + u), u, k0, KC, w_out, i * (8 * P) + e * 4 * P, 4 * P)
            ffn(1)
            y_dram = io["y"][0].rearrange("(b p) n -> p b n", p=P)
            for b in range(TB):
                sp.wait_ge(y_scaled_out, b + 1)
                sp.dma_start(y_dram[:, b, :], TOKS[:, b, :]).then_inc(stored, 16)
            sp.wait_ge(stored, 16 * TB)

        @block.gpsimd
        def _(pool):
            done = {"term": 0, "added": 0}

            def square(a, first):
                if first:
                    pool.tensor_tensor(SQ[:], a, a, ALU.mult).then_inc(sq_added, 1)
                else:
                    pool.wait_ge(sq_added, done["added"])
                    pool.tensor_tensor(SQT[:], a, a, ALU.mult).then_inc(sq_term, 1)
                    done["term"] += 1
                    pool.wait_ge(sq_term, done["term"])
                    pool.tensor_tensor(SQ[:], SQ[:], SQT[:], ALU.add).then_inc(sq_added, 1)
                done["added"] += 1

            def residual_squares(m, update, st):
                pool.wait_ge(x_updated, update + 1)
                for half in range(2):
                    if m == 0 and half == 0 and st > 0:
                        pool.wait_ge(stat_done, st)
                    t = 4 * m + 2 * half
                    square(X[:, t:t + 2, :], m == 0 and half == 0)

            pool.memset(ONES[:], 1.0).then_inc(ones_ready, 1)
            pool.memset(EPST[:], EPS).then_inc(ones_ready, 1)
            for m in range(4):
                residual_squares(m, m, ST_FFN1)

            steps = [0]

            def step(ins):
                ins.then_inc(rope_step, 1)
                steps[0] += 1
                pool.wait_ge(rope_step, steps[0])

            chunk, A, K = pi_chunks(), TAB[:, 1, :], [TAB[:, 2, :], TAB[:, 3, :], TAB[:, 4, :]]
            pool.wait_ge(pos_loaded, 16)
            pool.wait_ge(consts_loaded, 32)
            step(pool.tensor_copy(A, TAB[:, 0, :].bitcast(I32)))
            step(pool.tensor_scalar(A, A, FREQ[:, 0:1], None, ALU.mult))

            def turns(k, scale):
                step(pool.tensor_scalar(K[k], A, 1.0 / (TWO_PI * scale), MAGIC, ALU.mult, ALU.add))
                step(pool.tensor_scalar(K[k], K[k], MAGIC, None, ALU.subtract))

            def take(k, c, scale):
                step(pool.tensor_scalar(TAB[:, 6, :], K[k], chunk[c] * scale, None, ALU.mult))
                step(pool.tensor_tensor(A, A, TAB[:, 6, :], ALU.subtract))

            big, mid = 2.0 ** 24, 2.0 ** 12
            turns(0, big)
            take(0, 0, big)
            take(0, 1, big)
            turns(1, mid)
            take(1, 0, mid)
            take(0, 2, big)
            take(1, 1, mid)
            turns(2, 1.0)
            for k, c, s in ((2, 0, 1.0), (1, 2, mid), (2, 1, 1.0), (0, 3, big), (1, 3, mid), (2, 2, 1.0), (2, 3, 1.0)):
                take(k, c, s)
            turns(0, 1.0)
            for c in range(3):
                take(0, c, 1.0)
            pi32 = 3.1415925
            pool.tensor_scalar(A, A, pi32, -pi32, ALU.min, ALU.max).then_inc(rope_step, 1)
            pool.wait_ge(sin_ready, 2)
            step_n = steps[0] + 1
            pool.tensor_scalar(SIN[:], SIN[:], FREQ[:, 1:2], None, ALU.mult).then_inc(trig_ready, 1)
            pool.tensor_tensor(COS[:], TAB[:, 5, :], TAB[:, 5, :], ALU.mult).then_inc(rope_step, 1)
            pool.wait_ge(rope_step, step_n + 1)
            pool.tensor_scalar(COS[:], COS[:], -2.0, 1.0, ALU.mult, ALU.add).then_inc(trig_ready, 1)
            pool.memset(U[:, :, 0:PAD], 0.0).then_inc(pads_ready, 1)
            pool.memset(U[:, :, PAD + TOK:], 0.0).then_inc(pads_ready, 1)

            def hidden_lo(q, tile, w=2):
                pool.wait_ge(h_hi_ready, q + 1)
                pool.tensor_tensor(H[:, ds(tile, w), TOK:], HID[:, 0:w, :], f32(H[:, ds(tile, w), 0:TOK]),
                                   ALU.subtract).then_inc(h_lo_ready, 1)

            def ffn(f):
                for p, (_, nt) in enumerate(PARTS):
                    _, _, q0, x0 = part_start(f, p)
                    with pool.Fori(0, FULL_PAIRS[p]) as i:
                        hidden_lo(i + q0, i * 2)
                    if nt % 2:
                        hidden_lo(q0 + FULL_PAIRS[p], nt - 1, 1)
                for m in range(4):
                    residual_squares(m, x0 + m, (ST_MIX, ST_OUT)[f])

            ffn(0)

            order = [("mul", 0), ("mul", 1)]
            for k in range(1, TAPS - 1):
                order += [("mul", k + 1), ("add", k)]
            order.append(("add", TAPS - 1))
            step_of = {o: n + 1 for n, o in enumerate(order)}
            product = [SQT[:, 0, :], SQT[:, 1, :], HID[:, 1, :]]

            def conv(j, c):
                t, start = CONV_POOL[j], POOL_STEPS * j
                if c == 0:
                    pool.wait_ge(u_ready, t // 2 + 1)
                    pool.wait_ge(pads_ready, 2)
                    pool.wait_ge(taps_ready, 1)
                    pool.wait_ge(sq_added, done["added"])
                for what, k in order[16 * c:16 * c + 16]:
                    if what == "mul":
                        u, tap = window_of(t, k)
                        if k == 0:
                            ins = pool.tensor_scalar(Y[:, t, :], u, tap, gain("dw_bias", t), ALU.mult, ALU.add)
                        else:
                            if k >= 4:
                                pool.wait_ge(conv_pool, start + step_of["add", k - 3])
                            elif j:
                                pool.wait_ge(conv_pool, start)
                            ins = pool.tensor_scalar(product[k % 3], u, tap, None, ALU.mult)
                    else:
                        pool.wait_ge(conv_pool, start + max(step_of["mul", k], step_of.get(("add", k - 1), 1)))
                        ins = pool.tensor_tensor(Y[:, t, :], Y[:, t, :], product[k % 3], ALU.add)
                    ins.then_inc(conv_pool, 1)

            for j in range(GLU_PAIRS):
                pool.wait_ge(banks_free, MIX_G + j + 1)
                pool.wait_ge(rinv_ready, ST_MIX + 1)
                pool.tensor_tensor(SUM[:], SUM[:], over(RINV[:], 4), ALU.mult).then_inc(glu_scaled, 1)
                pool.wait_ge(sig_ready, j + 1)
                pool.tensor_tensor(U[:, 2 * j:2 * j + 2, PAD:PAD + TOK], SUM[:, 0:2, :], GATE[:],
                                   ALU.mult).then_inc(u_ready, 1)
                for q in ((0, 1), (2, 3), (4, 5), (6,))[j]:
                    conv(q // 4, q % 4)
            pool.wait_ge(kv_scaled, 1)
            pool.wait_ge(stat_done, ST_KV)
            square(SUM[:, 0:2, :], True)
            pool.tensor_tensor(KPSQ[:], SUM[0:ROPE, 2, :], SUM[0:ROPE, 2, :], ALU.mult).then_inc(kpe_sq, 1)
            conv(1, 3)
            pool.wait_ge(zq_scaled, 1)
            pool.wait_ge(stat_done, ST_ZQ)
            square(SUM[:, 0:2, :], True)
            square(SUM[:, 2:4, :], False)
            for c in range(4):
                conv(2, c)
            pool.wait_ge(conv_dve, CONV_DVE_END)
            pool.wait_ge(conv_pool, CONV_POOL_END)
            pool.wait_ge(stat_done, ST_CONV)
            for t in range(0, CT, 2):
                square(Y[:, t:t + 2, :], t == 0)
            pool.wait_ge(rinv_ready, ST_CONV + 1)
            pool.tensor_tensor(Y[:], Y[:], over(RINV2[:], CT), ALU.mult).then_inc(y_scaled, 1)
            for m in range(4):
                residual_squares(m, MIX_X + m, ST_FFN2)
            ffn(1)

        @block.scalar
        def _(act):
            uq_units = [0]

            def split(n, c, w=UNIT):
                act.wait_ge(sem_raw[c % 2], loads_by(n, c, uq_units[0]))
                if not (isinstance(n, int) and n < 2):
                    act.wait_ge(units_used, n - 1)
                act.activation(WHI[:, c % 2, 0:w], RAW[:, c % 2, 0:w], ACT.Copy).then_inc(whi_ready, 1)

            def losum(g, s, used, nt=4):
                act.wait_ge(units_used, used)
                if not (isinstance(g, int) and g < 1):
                    act.wait_ge(banks_free, g)
                act.activation(LOSUM[:, 0:nt, :], PS[:, 4 * s:4 * s + nt, TOK:], ACT.Copy).then_inc(losum_ready, 1)

            def silu(q, w=2):
                act.wait_ge(scaled, q + 1)
                act.activation(GATE[:, 0:w, :], SUM[:, 0:w, :], ACT.Silu).then_inc(gate_ready, 1)

            def hidden_hi(q, tile, w=2):
                act.wait_ge(hid_ready, q + 1)
                act.activation(H[:, ds(tile, w), 0:TOK], HID[:, 0:w, :], ACT.Copy).then_inc(h_hi_ready, 1)

            def residual_hi(m, update, name, idx):
                act.wait_ge(x_updated, update + 1)
                for t in range(4 * m, 4 * m + 4):
                    act.activation(XN[:, t, 0:TOK], X[:, t, :], ACT.Copy, scale=gain(name, t)).then_inc(x_hi_ready, 1)

            def root(st, src, dst, scale, also=None):
                act.wait_ge(stat_done, st + 1)
                if st:
                    act.wait_ge(rinv_ready, st)
                act.activation(dst, src, ACT.Sqrt, scale=scale, bias=EPST[:, 0:1]).then_inc(root_ready, 1)

            def no():
                pass

            x_dram = io["x"][0].rearrange("(b p) n -> p b n", p=P)
            act.dma_start(IDENT[:], io["ident"]).then_inc(ident_loaded, 16)
            for h in range(2):
                for b in range(TB):
                    act.dma_start(TOKS[:, b, h * (DM // 2):(h + 1) * (DM // 2)],
                                  x_dram[:, b, h * (DM // 2):(h + 1) * (DM // 2)]).then_inc((x_loaded_0, x_loaded_1)[h], 16)
            for name, n in GAIN_ROWS:
                at = GAIN_AT[name]
                act.dma_start(GROWS[at:at + n, :], io[name][0].rearrange("(t p) -> t p", p=P)).then_inc(gains_loaded, 16)
            for name, plain, rot in (("q_head_norm", G_QN, G_QR), ("k_head_norm", G_KN, G_KR)):
                act.dma_start(GROWS[plain:plain + 1, :], io[name][:, 0:NOPE]).then_inc(gains_loaded, 16)
                for e in range(2):
                    act.dma_start(GROWS[rot:rot + 1, e * ROPE:(e + 1) * ROPE],
                                  io[name][:, NOPE:QK]).then_inc(gains_loaded, 16)
            act.dma_start(SEL[:], io["sel"]).then_inc(consts_loaded, 16)
            act.dma_start(FREQ[:], io["freq"]).then_inc(consts_loaded, 16)
            act.dma_start(TAPR, io["dw_kernel"][0]).then_inc(taps_loaded, 16)
            act.dma_start(TAB[:, 0, :].bitcast(I32),
                          io["positions"][0].partition_broadcast(P)).then_inc(pos_loaded, 16)
            split(0, 0)
            split(1, 1)
            act.wait_ge(gains_turned, 1)
            act.activation(GAIN[:], PS[:, 7, 0:GAINS], ACT.Copy).then_inc(gains_ready, 1)
            act.wait_ge(gains_ready, 1)
            for m in range(4):
                residual_hi(m, m, "ffn1_norm", m)

            def taps_and_root():
                act.wait_ge(taps_turned, 1)
                act.activation(TAPW[:], PS[:, 6, 0:CT * TAPS], ACT.Copy).then_inc(taps_ready, 1)
                root(ST_FFN1, PS[:, 4, 0:TOK], ROOT[:], 1.0 / DM)

            def sines():
                act.wait_ge(rope_step, ROPE_STEPS)
                act.activation(SIN[:], TAB[:, 1, :], ACT.Sin).then_inc(sin_ready, 1)
                act.activation(TAB[:, 5, :], TAB[:, 1, :], ACT.Sin, scale=0.5).then_inc(sin_ready, 1)

            def window(n, jobs, w=UNIT, count=KC, skip=0):
                for c in range(skip, count):
                    split(n + c, c, w)
                    if 0 < c <= len(jobs):
                        jobs[c - 1]()

            def ffn(f, before, extra):
                for p, (_, nt) in enumerate(PARTS):
                    n, g, q0, x0 = part_start(f, p)
                    du = DOWN_UNITS[p]

                    def pair_jobs(q, g, s, used, tile, w=2):
                        return [lambda: losum(g, s, used, 2 * w), lambda: silu(q, w), lambda: hidden_hi(q, tile, w)]

                    if f == p == 0:
                        window(n, [], skip=2)
                        extra()
                    else:
                        window(n, before + [extra if p == 0 else no])
                    s0 = g % 2
                    window(n + KC, pair_jobs(q0, g, s0, n + KC, 0))
                    if f == p == 0:
                        sines()
                    with act.Fori(1, FULL_PAIRS[p] // 2) as i:
                        for e in range(2):
                            window(i * (2 * KC) + (n + KC * e),
                                   pair_jobs(i * 2 + (q0 + e - 1), i * 2 + (g + e - 1), (s0 + e + 1) % 2,
                                             i * (2 * KC) + (n + KC * e), i * 4 + (2 * e - 2)))
                    for q in range(FULL_PAIRS[p] // 2 * 2, PAIR_COUNT[p]):
                        window(n + KC * q, pair_jobs(q0 + q - 1, g + q - 1, (s0 + q + 1) % 2, n + KC * q, 2 * q - 2),
                               KC * 2 * P * min(2, nt - 2 * q))
                    n, g = n + KC * PAIR_COUNT[p], g + PAIR_COUNT[p]
                    last = nt - 2 * (PAIR_COUNT[p] - 1)
                    jobs = pair_jobs(q0 + PAIR_COUNT[p] - 1, g - 1, (g - 1) % 2, n, nt - last, last)
                    for m in range(4):
                        for u in range(du):
                            split(n + du * m + u, du * m + u, 4 * P * min(KC, nt - KC * u))
                            if u:
                                jobs[u - 1]()
                        if du == 3 and len(jobs) > 2:
                            jobs[2]()
                        jobs = [lambda m=m, g=g, n=n, du=du: losum(g + m, (g + m) % 2, n + du * (m + 1)), no, no]
                        if p == 2 and f == 0:
                            jobs[1] = lambda m=m, x0=x0: residual_hi(m, x0 + m, "mix_norm", 4 + m)
                        if p == 2 and f == 1:
                            jobs[1] = lambda m=m, x0=x0: final_gain(m, x0 + m)
                            jobs[2] = lambda m=m, g=g: final_copy(m, (g + m) % 2)
                    before = jobs[0:2]
                return jobs

            def final_gain(m, update):
                act.wait_ge(x_updated, update + 1)
                if m:
                    act.wait_ge(y_turned, m)
                for t in range(4):
                    act.activation(YG[:, t, :], X[:, 4 * m + t, :], ACT.Copy,
                                   scale=gain("final_norm", 4 * m + t)).then_inc(y_gained, 1)

            def final_copy(m, s):
                act.wait_ge(y_turned, m + 1)
                act.activation(TOKS[:, :, 4 * m * P:4 * (m + 1) * P], PS[:, 4 * s:4 * s + TB, :], ACT.Copy).then_inc(y_copied, 1)

            jobs = ffn(0, [], taps_and_root)

            def glu_jobs(j):
                def sigmoid():
                    act.wait_ge(glu_scaled, j + 1)
                    act.activation(GATE[:], SUM[:, 2:4, :], ACT.Sigmoid).then_inc(sig_ready, 1)
                return [lambda: losum(MIX_G + j, j % 2, MIX_N + KC * (j + 1)), sigmoid]

            window(MIX_N, [jobs[0], jobs[1], lambda: root(ST_MIX, PS[:, 4, 0:TOK], ROOT[:], 1.0 / DM)])
            for j in range(1, GLU_PAIRS):
                window(MIX_N + KC * j, glu_jobs(j - 1))
            window(MIX_N + 16, glu_jobs(GLU_PAIRS - 1), KC * (KVR + ROPE))

            def kv_losum():
                act.wait_ge(units_used, MIX_N + 20)
                act.wait_ge(banks_free, KV_G)
                act.activation(LOSUM[:, 0:2, :], PS[:, 0:2, TOK:], ACT.Copy).then_inc(losum_ready, 1)
                act.activation(LOSUM[0:ROPE, 2, :], PS[0:ROPE, 2, TOK:], ACT.Copy).then_inc(losum_ready, 1)

            def kpe_moves():
                act.wait_ge(kpe_gained, 1)
                h = ROPE // 2
                for dst, d0, s0, n in ((KG, ROPE, 0, ROPE), (KSW, 0, h, h), (KSW, h, 0, h),
                                       (KSW, ROPE, h, h), (KSW, ROPE + h, 0, h)):
                    act.activation(dst[d0:d0 + n, :], KG[s0:s0 + n, :], ACT.Copy).then_inc(kpe_moved, 1)

            def latent_hi(count, ready, n, dst, name):
                act.wait_ge(ready, 1)
                for t in range(n):
                    act.activation(dst[:, t, 0:TOK], SUM[:, t, :], ACT.Copy, scale=gain(name, t)).then_inc(count, 1)

            split(MIX_N + 20, 0)
            split(MIX_N + 21, 1)
            kv_losum()
            split(MIX_N + 22, 0)
            kpe_moves()
            split(MIX_N + 23, 1)
            root(ST_KV, PS[:, 0, 0:TOK], ROOT[:], 1.0 / KVR)
            latent_hi(kv_hi, kv_normed, KVR // P, H[:, 16:18], "kv_norm")
            split(MIX_N + 24, 0, 1024)
            losum(ZQ_G, 1, MIX_N + 24)
            split(MIX_N + 25, 1, 1024)
            split(MIX_N + 26, 0, 1024)
            root(ST_ZQ, PS[:, 4, 0:TOK], ROOT[:], 1.0 / QR)
            act.wait_ge(units_used, MIX_N + 26)
            act.wait_ge(banks_free, V_G)
            act.wait_ge(taps_turned, 1)
            act.activation(V[:, :, :].rearrange("p b (h n) -> p (b h) n", n=512), PS[:, 0:4, :],
                           ACT.Copy).then_inc(banks_free, 1)
            split(MIX_N + 27, 1, 1024)
            latent_hi(zq_hi, zq_normed, QR // P, XN, "q_norm")
            losum(K_G, 1, MIX_N + 27)
            uq_units[0] = 1
            split(MIX_N + 28, 0)
            losum(K_G + 1, 0, MIX_N + 28)
            split(MIX_N + 29, 1)
            losum(Q_G, 1, MIX_N + 29)
            uq_units[0] = 2
            split(MIX_N + 30, 0, 1024)
            losum(Q_G + 1, 0, MIX_N + 30)
            split(MIX_N + 31, 1, 1024)
            losum(R_G, 1, MIX_N + 31, 2)
            split(MIX_N + 32, 0)
            losum(R_G + 1, 0, MIX_N + 32, 2)
            split(MIX_N + 33, 1)
            for i, src in enumerate((KN[:, 0:4], KN[:, 4:8], QN[:, 0:4], QN[:, 4:8], QROT)):
                act.wait_ge(banks_free, K_G + (i + 1 if i < 4 else 6))
                if i >= 2:
                    act.wait_ge(hstat_done, i - 1)
                act.activation((SQB, SUM[:])[i % 2], src, ACT.Square).then_inc(hsq_ready, 1)
                if i == 3:
                    act.wait_ge(hstat_done, 2)
                    act.activation(ROOT[0:HEADS, :], PS[0:HEADS, 6, 0:TOK], ACT.Sqrt, scale=1.0 / QK,
                                   bias=EPST[0:HEADS, 0:1]).then_inc(kroot_ready, 1)
            act.wait_ge(banks_free, R_G + 2)
            act.activation(LOSUM[:], QROT, ACT.Copy, scale=GAIN[:, G_QR:G_QR + 1]).then_inc(qrot_gained, 1)
            act.wait_ge(qrot_gained, 1)
            act.wait_ge(hstat_done, 4)
            h = ROPE // 2
            for d in range(4):
                src = d ^ 1
                act.activation(SUM[d * h:(d + 1) * h], LOSUM[src * h:(src + 1) * h], ACT.Copy).then_inc(qrot_moved, 1)
            act.wait_ge(hstat_done, 5)
            act.activation(QSTAT[:, 0, :], PS[:, 7, 16:32], ACT.Copy).then_inc(qstat_copied, 1)
            act.wait_ge(qstat_sum, 1)
            act.activation(QSTAT[:, 2, :], QSTAT[:, 1, :], ACT.Sqrt, scale=1.0 / QK,
                           bias=EPST[:, 0:1]).then_inc(qroot_ready, 1)
            root(ST_CONV, PS[:, 5, 0:TOK], ROOT[:], 1.0 / CONV)
            act.wait_ge(conv_dve, CONV_DVE_END)
            act.wait_ge(conv_pool, CONV_POOL_END)
            act.dma_start(EXPAND, io["expand"]).then_inc(expand_loaded, 16)

            act.wait_ge(qkg_ready, 1)
            act.wait_ge(k_scaled, HEADS)
            with act.Fori(0, HEADS // 2) as i:
                for e in range(2):
                    act.wait_ge(o_done, i * 2 + 1)
                    act.activation(QS[:, e, :], QN[:, ds(i * 2 + e, 1), :], ACT.Copy,
                                   scale=QKG[:, 0:1]).then_inc(q_static, 1)
                for e in range(2):
                    r = slice(e * ROPE, (e + 1) * ROPE)
                    act.activation(QRS[e][r, :].unsqueeze(1), QROT[r, ds(i, 1), :], ACT.Copy).then_inc(qr_static, 1)
                for e in range(2):
                    act.wait_ge(bias_ready, i * 2 + (e + 1))
                    for b in range(TB):
                        act.activation(PB[:, e, b, :], PS[:, e, b * TOK:(b + 1) * TOK], ACT.Exp,
                                       bias=SMALL[:, e, 1, b:b + 1], scale=QRMS[:, 1, ds(i * 2 + (e + 8 * b), 1)],
                                       accum_out=SMALL[:, e, 2, b:b + 1]).then_inc(exp_ready, 1)
                for e in range(2):
                    act.wait_ge(probs_turned, i * 2 + (e + 1))
                    act.activation(PT[e][:], PS[:, 2 + e, :], ACT.Copy).then_inc(probsT_ready, 1)
                for e in range(2):
                    act.wait_ge(o_done, i * 2 + (e + 2))
                    act.activation(H[:, ds(i * 2 + (8 + e), 1), 0:TOK], PS[:, 4 + e, 0:TOK],
                                   ACT.Copy).then_inc(o_hi_ready, 1)
            act.wait_ge(y_scaled, 1)
            for t in range(CT):
                act.activation(Y[:, t, :], Y[:, t, :], ACT.Silu, scale=gain("conv_norm", t)).then_inc(y_silu, 1)
            act.wait_ge(y_silu, CT)
            act.activation(H[:, 0:CT, 0:TOK], Y[:], ACT.Copy).then_inc(a_hi_ready, 1)

            jobs = []
            for m in range(4):
                window(WO_N + KC * m, jobs, skip=2 if m == 0 else 0)
                jobs = [lambda m=m: losum(WO_G + m, (WO_G + m) % 2, WO_N + KC * (m + 1)),
                        lambda m=m: residual_hi(m, MIX_X + m, "ffn2_norm", 8 + m)]
            jobs = ffn(1, jobs, lambda: root(ST_FFN2, PS[:, STAT_BANK[1], 0:TOK], ROOT[:], 1.0 / DM))
            for job in jobs:
                job()
            act.wait_ge(stat_done, ST_OUT + 1)
            act.activation(YSTAT[:, 0, :], PS[:, 3, 0:TB], ACT.Sqrt, scale=1.0 / DM,
                           bias=EPST[:, 0:1]).then_inc(root_ready, 1)

        @block.vector
        def _(dve):
            def split(n, c, w=UNIT):
                dve.wait_ge(whi_ready, n + 1)
                dve.tensor_tensor(WLO[:, c % 2, 0:w], RAW[:, c % 2, 0:w], f32(WHI[:, c % 2, 0:w]),
                                  ALU.subtract).then_inc(wlo_ready, 1)

            def window(n, jobs, w=UNIT, skip=0):
                for c in range(skip, KC):
                    split(n + c, c, w)
                    if 0 < c <= len(jobs):
                        jobs[c - 1]()

            def no():
                pass

            def add_halves(g, s, nt, dst, count=None):
                dve.wait_ge(losum_ready, g + 1 if count is None else count)
                dve.tensor_tensor(dst, PS[:, 4 * s:4 * s + nt, 0:TOK], LOSUM[:, 0:nt, :], ALU.add).then_inc(banks_free, 1)

            def pair_sums(q, g, s, stat, w=2):
                add_halves(g, s, 2 * w, SUM[:, 0:2 * w, :])
                dve.wait_ge(banks_free, g + 1)
                dve.wait_ge(rinv_ready, stat + 1)
                dve.tensor_tensor(SUM[:, 0:2 * w, :], SUM[:, 0:2 * w, :], over(RINV[:], 2 * w), ALU.mult).then_inc(scaled, 1)

            def hidden(q, w=2):
                dve.wait_ge(gate_ready, q + 1)
                if not (isinstance(q, int) and q < 1):
                    dve.wait_ge(h_lo_ready, q)
                dve.tensor_tensor(HID[:, 0:w, :], GATE[:, 0:w, :], SUM[:, w:2 * w, :], ALU.mult).then_inc(hid_ready, 1)

            def residual_add(g, m, scale):
                add_halves(g, g % 2, 4, SUM[:])
                dve.wait_ge(banks_free, g + 1)
                xs = X[:, 4 * m:4 * m + 4, :]
                dve.scalar_tensor_tensor(out=xs, in0=SUM[:], scalar=scale, in1=xs,
                                         op0=ALU.mult, op1=ALU.add).then_inc(x_updated, 1)

            def residual_lo(m, name, idx):
                for t in range(4):
                    k = 4 * m + t
                    dve.wait_ge(x_hi_ready, 4 * idx + t + 1)
                    dve.scalar_tensor_tensor(out=XN[:, k, TOK:], in0=X[:, k, :], scalar=gain(name, k),
                                             in1=f32(XN[:, k, 0:TOK]), op0=ALU.mult,
                                             op1=ALU.subtract).then_inc(x_lo_ready, 1)

            def inverse(st, dst):
                dve.wait_ge(root_ready, st + 1)
                dve.reciprocal(dst, ROOT[:]).then_inc(rinv_ready, 1)

            def ffn(f, before, stat):
                for p, (_, nt) in enumerate(PARTS):
                    n, g, q0, x0 = part_start(f, p)
                    du, s0 = DOWN_UNITS[p], g % 2

                    def pair_jobs(q, g, s, w=2):
                        return [lambda: pair_sums(q, g, s, stat, w), lambda: hidden(q, w)]

                    if f == p == 0:
                        window(n, [], skip=2)
                        inverse(stat, RINV[:])
                    else:
                        window(n, before + [lambda: inverse(stat, RINV[:]) if p == 0 else no()])
                    window(n + KC, pair_jobs(q0, g, s0))
                    with dve.Fori(1, FULL_PAIRS[p] // 2) as i:
                        for e in range(2):
                            window(i * (2 * KC) + (n + KC * e),
                                   pair_jobs(i * 2 + (q0 + e - 1), i * 2 + (g + e - 1), (s0 + e + 1) % 2))
                    for q in range(FULL_PAIRS[p] // 2 * 2, PAIR_COUNT[p]):
                        window(n + KC * q, pair_jobs(q0 + q - 1, g + q - 1, (s0 + q + 1) % 2),
                               KC * 2 * P * min(2, nt - 2 * q))
                    n, g = n + KC * PAIR_COUNT[p], g + PAIR_COUNT[p]
                    last = nt - 2 * (PAIR_COUNT[p] - 1)
                    jobs = pair_jobs(q0 + PAIR_COUNT[p] - 1, g - 1, (g - 1) % 2, last)
                    for m in range(4):
                        for u in range(du):
                            split(n + du * m + u, du * m + u, 4 * P * min(KC, nt - KC * u))
                            if 0 < u <= len(jobs):
                                jobs[u - 1]()
                        jobs = [lambda m=m, g=g: residual_add(g + m, m, 0.5), no]
                        if p == 2 and f == 0:
                            jobs[1] = lambda m=m: residual_lo(m, "mix_norm", 4 + m)
                    before = jobs
                return jobs

            split(0, 0)
            split(1, 1)
            for m in range(4):
                dve.wait_ge(x_turned, m + 1)
                dve.tensor_copy(X[:, 4 * m:4 * m + 4, :].rearrange("p t n -> p (t n)"),
                                PS[:, 2 * m:2 * m + 2, :].rearrange("p b n -> p (b n)")).then_inc(x_updated, 1)
                dve.wait_ge(x_updated, m + 1)
                dve.wait_ge(gains_ready, 1)
                residual_lo(m, "ffn1_norm", m)
            dve.tensor_tensor(QKG[:], GAIN[:, G_QN:G_QN + 1], GAIN[:, G_KN:G_KN + 1], ALU.mult).then_inc(qkg_ready, 1)
            jobs = ffn(0, [], ST_FFN1)

            def conv(j, c):
                t, start, acc2 = CONV_DVE[j], DVE_STEPS * j, HID[:, 0, :]
                if c == 0:
                    dve.wait_ge(u_ready, t // 2 + 1)
                    dve.wait_ge(pads_ready, 2)
                    dve.wait_ge(taps_ready, 1)
                for k in range(8 * c, 8 * c + 8):
                    acc = acc2 if k % 2 else Y[:, t, :]
                    if k == TAPS:
                        dve.wait_ge(conv_dve, start + k)
                        ins = dve.tensor_tensor(Y[:, t, :], Y[:, t, :], acc2, ALU.add)
                    elif k == 0:
                        u, tap = window_of(t, k)
                        ins = dve.tensor_scalar(acc, u, tap, gain("dw_bias", t), ALU.mult, ALU.add)
                    elif k == 1:
                        if j:
                            dve.wait_ge(conv_dve, start)
                        u, tap = window_of(t, k)
                        ins = dve.tensor_scalar(acc, u, tap, None, ALU.mult)
                    else:
                        u, tap = window_of(t, k)
                        dve.wait_ge(conv_dve, start + k - 1)
                        ins = dve.scalar_tensor_tensor(out=acc, in0=u, scalar=tap, in1=acc, op0=ALU.mult, op1=ALU.add)
                    ins.then_inc(conv_dve, 1)

            def glu_sums(j):
                if j:
                    dve.wait_ge(u_ready, j)
                add_halves(MIX_G + j, j % 2, 4, SUM[:])

            def scale_by(dst, r, count):
                dve.tensor_tensor(dst, dst, r, ALU.mult).then_inc(count, 1)

            window(MIX_N, jobs + [lambda: inverse(ST_MIX, RINV[:])])
            for j in range(1, GLU_PAIRS + 1):
                for c in range(KC):
                    split(MIX_N + KC * j + c, c, UNIT if j < GLU_PAIRS else KC * (KVR + ROPE))
                    if c == 1:
                        glu_sums(j - 1)
                    if j >= 2:
                        conv(j - 2, c)
            split(MIX_N + 20, 0)
            conv(3, 0)
            split(MIX_N + 21, 1)
            dve.wait_ge(u_ready, GLU_PAIRS)
            dve.wait_ge(losum_ready, KV_G + 2)
            dve.tensor_tensor(SUM[:, 0:2, :], PS[:, 0:2, 0:TOK], LOSUM[:, 0:2, :], ALU.add)
            dve.tensor_tensor(SUM[0:ROPE, 2, :], PS[0:ROPE, 2, 0:TOK], LOSUM[0:ROPE, 2, :], ALU.add).then_inc(banks_free, 1)
            dve.wait_ge(banks_free, KV_G + 1)
            dve.tensor_tensor(SUM[:, 0:2, :], SUM[:, 0:2, :], over(RINV[:], 2), ALU.mult)
            scale_by(SUM[0:ROPE, 2, :], RINV[0:ROPE, :], kv_scaled)
            dve.wait_ge(kv_scaled, 1)
            dve.tensor_scalar(KG[0:ROPE, :], SUM[0:ROPE, 2, :], GAIN[0:ROPE, G_KR:G_KR + 1], None,
                              ALU.mult).then_inc(kpe_gained, 1)
            conv(3, 1)
            split(MIX_N + 22, 0)
            conv(3, 2)
            split(MIX_N + 23, 1)
            inverse(ST_KV, RINV2[:])
            dve.wait_ge(rinv_ready, ST_KV + 1)
            scale_by(SUM[:, 0:2, :], over(RINV2[:], 2), kv_normed)
            dve.wait_ge(kpe_moved, 5)
            dve.wait_ge(trig_ready, 2)
            dve.tensor_tensor(KROT[:], KG, COS[:], ALU.mult).then_inc(kpe_mixed, 1)
            scale_by(KSW, SIN[:], kpe_mixed)

            def latent_lo(count, hi, normed, n, dst, name):
                dve.wait_ge(normed, 1)
                for t in range(n):
                    dve.wait_ge(hi, t + 1)
                    dve.scalar_tensor_tensor(out=dst[:, t, TOK:], in0=SUM[:, t, :], scalar=gain(name, t),
                                             in1=f32(dst[:, t, 0:TOK]), op0=ALU.mult, op1=ALU.subtract).then_inc(count, 1)

            latent_lo(kv_lo, kv_hi, kv_normed, KVR // P, H[:, 16:18], "kv_norm")
            dve.wait_ge(kpe_mixed, 2)
            dve.tensor_tensor(KROT[:], KROT[:], KSW, ALU.add).then_inc(krot_ready, 1)
            split(MIX_N + 24, 0, 1024)
            dve.wait_ge(kpe_sq, 1)
            dve.wait_ge(kv_lo, KVR // P)
            add_halves(ZQ_G, 1, 4, SUM[:], ZQ_G + 2)
            dve.wait_ge(banks_free, ZQ_G + 1)
            scale_by(SUM[:], over(RINV[:], 4), zq_scaled)
            split(MIX_N + 25, 1, 1024)
            conv(3, 3)
            split(MIX_N + 26, 0, 1024)
            inverse(ST_ZQ, RINV2[:])
            dve.wait_ge(rinv_ready, ST_ZQ + 1)
            scale_by(SUM[:], over(RINV2[:], 4), zq_normed)
            split(MIX_N + 27, 1, 1024)
            latent_lo(zq_lo, zq_hi, zq_normed, QR // P, XN, "q_norm")
            add_halves(K_G, 1, 4, KN[:, 0:4, :])
            split(MIX_N + 28, 0)
            add_halves(K_G + 1, 0, 4, KN[:, 4:8, :])
            split(MIX_N + 29, 1)
            conv(4, 0)
            add_halves(Q_G, 1, 4, QN[:, 0:4, :])
            split(MIX_N + 30, 0, 1024)
            conv(4, 1)
            add_halves(Q_G + 1, 0, 4, QN[:, 4:8, :])
            split(MIX_N + 31, 1, 1024)
            conv(4, 2)
            add_halves(R_G, 1, 2, QROT[:, 0:2, :])
            split(MIX_N + 32, 0)
            add_halves(R_G + 1, 0, 2, QROT[:, 2:4, :])
            split(MIX_N + 33, 1)
            conv(4, 3)
            dve.wait_ge(kroot_ready, 1)
            dve.wait_ge(krot_ready, 1)
            dve.reciprocal(KRINV, ROOT[0:HEADS, :]).then_inc(krinv_ready, 1)
            dve.wait_ge(qrot_moved, 4)
            dve.tensor_tensor(QROT, LOSUM[:], over(COS[:], 4), ALU.mult).then_inc(qrot_mixed, 1)
            scale_by(SUM[:], over(SIN[:], 4), qrot_mixed)
            dve.wait_ge(qrot_mixed, 2)
            dve.tensor_tensor(QROT, QROT, SUM[:], ALU.add).then_inc(qrot_ready, 1)
            dve.wait_ge(qstat_copied, 1)
            dve.tensor_tensor(QSTAT[:, 1, :], PS[:, 7, 0:16], QSTAT[:, 0, :], ALU.add).then_inc(qstat_sum, 1)
            dve.wait_ge(qroot_ready, 1)
            dve.reciprocal(QRMS[:, 0, :], QSTAT[:, 2, :]).then_inc(qrinv_ready, 1)
            dve.wait_ge(qrinv_ready, 1)
            dve.tensor_scalar(QRMS[:, 1, :], QRMS[:, 0, :], SCALE, None, ALU.mult).then_inc(qscale_ready, 1)
            dve.tensor_scalar(QSTAT[:, 3, :], QRMS[:, 0, :], -SCALE, None, ALU.mult).then_inc(qscale_ready, 1)
            inverse(ST_CONV, RINV2[:])
            dve.wait_ge(conv_pool, CONV_POOL_END)
            dve.wait_ge(conv_dve, CONV_DVE_END)
            for j in range(HEADS // 2):
                if j < HEADS // 2 - 1:
                    dve.wait_ge(kbcast_done, j + 1)
                else:
                    dve.wait_ge(o_done, 1)
                dve.tensor_tensor(KN[:, 2 * j:2 * j + 2, :], KN[:, 2 * j:2 * j + 2, :],
                                  PS[:, j, :].rearrange("p (e n) -> p e n", e=2), ALU.mult)
                for e in range(2):
                    r = slice(e * ROPE, (e + 1) * ROPE)
                    dve.tensor_tensor(KRH[r, j, :], KROT[r, :], PS[r, j, e * TOK:(e + 1) * TOK],
                                      ALU.mult).then_inc(k_scaled, 1)
            dve.wait_ge(k_scaled, HEADS)
            dve.memset(QRS[0][ROPE:, :], 0.0).then_inc(qr_zeroed, 1)
            dve.memset(QRS[1][0:ROPE, :], 0.0).then_inc(o_lo_ready, 1)
            dve.wait_ge(banks_free, V_G + 1)
            with dve.Fori(0, HEADS // 2) as i:
                for e in range(2):
                    dve.wait_ge(o_done, i * 2 + 1)
                    dve.tensor_copy(VS[:, e, :, :], V[:, :, ds(i * (2 * VD) + e * VD, VD)]).then_inc(v_static, 1)
                for e in range(2):
                    dve.wait_ge(scores_done, i * 2 + (e + 1))
                    dve.reduce_max(SMALL[:, e, 0, :], PS[:, e, :].rearrange("p (b n) -> p b n", b=TB),
                                   AX.X).then_inc(max_ready, 1)
                    dve.wait_ge(max_ready, i * 2 + (e + 1))
                    dve.tensor_tensor(SMALL[:, e, 1, :].unsqueeze(2), SMALL[:, e, 0, :].unsqueeze(2),
                                      QSTAT[:, 3, :].rearrange("p (b h) -> p b h", b=TB)[:, :, ds(i * 2 + e, 1)],
                                      ALU.mult).then_inc(bias_ready, 1)
                for e in range(2):
                    dve.wait_ge(exp_ready, i * 4 + (2 * e + 2))
                    dve.reciprocal(SMALL[:, e, 3, :], SMALL[:, e, 2, :]).then_inc(den_ready, 1)
                    dve.wait_ge(den_ready, i * 2 + (e + 1))
                    for b in range(TB):
                        dve.tensor_scalar(PN[:, e, b, :], PB[:, e, b, :], SMALL[:, e, 3, b:b + 1], None,
                                          ALU.mult).then_inc(probs_ready, 1)
                for e in range(2):
                    dve.wait_ge(o_hi_ready, i * 2 + (e + 1))
                    dve.tensor_tensor(H[:, ds(i * 2 + (8 + e), 1), TOK:], PS[:, 4 + e, 0:TOK].unsqueeze(1),
                                      f32(H[:, ds(i * 2 + (8 + e), 1), 0:TOK]), ALU.subtract).then_inc(o_lo_ready, 1)
            dve.wait_ge(a_hi_ready, 1)
            dve.tensor_tensor(H[:, 0:CT, TOK:], Y[:], f32(H[:, 0:CT, 0:TOK]), ALU.subtract).then_inc(a_lo_ready, 1)
            jobs = []
            for m in range(4):
                window(WO_N + KC * m, jobs, skip=2 if m == 0 else 0)
                jobs = [lambda m=m: residual_add(WO_G + m, m, 1.0),
                        lambda m=m: residual_lo(m, "ffn2_norm", 8 + m)]
            jobs = ffn(1, jobs, ST_FFN2)
            jobs[0]()
            dve.wait_ge(root_ready, ST_OUT + 1)
            dve.reciprocal(YSTAT[:, 1, :], YSTAT[:, 0, :]).then_inc(rinv_ready, 1)
            dve.wait_ge(rinv_ready, ST_OUT + 1)
            dve.wait_ge(y_copied, 4)
            for b in range(TB):
                dve.tensor_scalar(TOKS[:, b, :], TOKS[:, b, :], YSTAT[:, 1, b:b + 1], None,
                                  ALU.mult).then_inc(y_scaled_out, 1)

        @block.tensor
        def _(pe):
            mm = pe.matmul

            def unit(n, c, banks, width, ks, rhs, k_first, k_last, widths=None):
                pe.wait_ge(wlo_ready, n + 1)
                s = c % 2
                for j, k in enumerate(ks):
                    for t, bank in enumerate(banks):
                        w = P if widths is None else widths[t]
                        at = j * width + t * P
                        first, last = k == k_first, k == k_last

                        def hi():
                            return mm(PS[0:w, bank, :], WHI[:, s, at:at + w], rhs(k), start=first, stop=last)

                        def lo():
                            return mm(PS[0:w, bank, 0:TOK], WLO[:, s, at:at + w], rhs(k)[:, 0:TOK],
                                      start=False, stop=False)

                        if last:
                            lo()
                            ins = hi()
                        else:
                            hi()
                            ins = lo()
                ins.then_inc(units_used, 1)

            def xn(k):
                return XN[:, k, :]

            def hid(k):
                return H[:, k, :]

            def free(g):
                if not (isinstance(g, int) and g < 2):
                    pe.wait_ge(banks_free, g - 1)

            def bank_set(s, n=4):
                return list(range(4 * s, 4 * s + n))

            def stat(st, bank):
                pe.wait_ge(sq_added, SQ_END[st])
                mm(PS[:, bank, 0:TOK], ONES[:], SQ[:, 0, :], start=True, stop=False)
                mm(PS[:, bank, 0:TOK], ONES[:], SQ[:, 1, :], start=False, stop=True).then_inc(stat_done, 1)

            def pair(n, g, s, w=2, first=0, hook=None, residual=None):
                free(g)
                for c in range(KC):
                    if residual is not None:
                        pe.wait_ge(x_lo_ready, residual + 4 * (c + 1))
                    if c == 3 and hook:
                        hook()
                    unit(n + c, c, bank_set(s, 2 * w), 2 * w * P, range(KC * c, KC * c + KC), xn, 0, DT - 1)

            def ffn(f, hook, residual):
                for p, (_, nt) in enumerate(PARTS):
                    n, g, q0, _ = part_start(f, p)
                    s0 = g % 2
                    pair(n, g, s0, hook=hook if p == 0 else None, residual=residual if p == 0 else None)
                    if p == 0:
                        pe.wait_ge(root_ready, (ST_FFN1, ST_FFN2)[f] + 1)
                        if f == 0:
                            pe.wait_ge(taps_ready, 1)
                    pair(n + KC, g + 1, 1 - s0)
                    with pe.Fori(1, FULL_PAIRS[p] // 2) as i:
                        for e in range(2):
                            pair(i * (2 * KC) + (n + KC * e), i * 2 + (g + e), (s0 + e) % 2)
                    for q in range(FULL_PAIRS[p] // 2 * 2, PAIR_COUNT[p]):
                        pair(n + KC * q, g + q, (s0 + q) % 2, min(2, nt - 2 * q))
                    n, g, du = n + KC * PAIR_COUNT[p], g + PAIR_COUNT[p], DOWN_UNITS[p]

                    def down(n, g, s, c0, turn=None):
                        free(g)
                        for u in range(du):
                            ks = range(KC * u, min(KC * u + KC, nt))
                            pe.wait_ge(h_lo_ready, q0 + (ks[-1] + 2) // 2)
                            if turn and u == du - 1:
                                turn()
                            unit(n + u, c0 + u, bank_set(s), 4 * P, ks, hid, 0, nt - 1)

                    if (f, p) == (1, 2):
                        for m in range(4):
                            if m >= 2:
                                pe.wait_ge(y_copied, m - 1)
                            down(n + du * m, g + m, (g + m) % 2, du * m,
                                 (lambda: turn_result(m - 1, g + m - 1)) if m else None)
                        return g + 3
                    with pe.Fori(0, 2) as i:
                        for e in range(2):
                            down(i * (2 * du) + (n + du * e), i * 2 + (g + e), (g + e) % 2, du * e)

            def turn_result(m, g):
                pe.wait_ge(banks_free, g + 1)
                pe.wait_ge(y_gained, 4 * (m + 1))
                for b in range(TB):
                    for t in range(4):
                        ins = pe.transpose(PS[:, 4 * (g % 2) + b, t * P:(t + 1) * P], YG[:, t, b * P:(b + 1) * P], IDENT[:])
                ins.then_inc(y_turned, 1)

            pe.wait_ge(ident_loaded, 16)

            def turn_x(m):
                for t in range(4):
                    for b in range(TB):
                        ins = pe.transpose(PS[:, 2 * m + t // 2, (t % 2) * TOK + b * P:(t % 2) * TOK + (b + 1) * P],
                                           TOKS[:, b, (4 * m + t) * P:(4 * m + t + 1) * P], IDENT[:])
                ins.then_inc(x_turned, 1)

            pe.wait_ge(x_loaded_0, 16 * TB)
            turn_x(0)
            turn_x(1)
            pe.wait_ge(x_loaded_1, 16 * TB)
            turn_x(2)
            pe.wait_ge(gains_loaded, 16 * (len(GAIN_ROWS) + 6))
            pe.transpose(PS[:, 7, 0:GAINS], GROWS, IDENT[0:GAINS, 0:GAINS]).then_inc(gains_turned, 1)
            pe.wait_ge(gains_ready, 1)
            turn_x(3)
            pe.wait_ge(ones_ready, 1)

            def taps_and_stat():
                pe.wait_ge(taps_loaded, 16)
                for t in range(CT):
                    ins = pe.transpose(PS[:, 6, t * TAPS:(t + 1) * TAPS], TAPR[:, t * P:(t + 1) * P],
                                       IDENT[0:TAPS, 0:TAPS])
                ins.then_inc(taps_turned, 1)
                stat(ST_FFN1, STAT_BANK[0])

            pe.wait_ge(x_updated, 4)
            ffn(0, taps_and_stat, 0)

            def mix_stat():
                pe.wait_ge(banks_free, MIX_G)
                stat(ST_MIX, 4)

            pair(MIX_N, MIX_G, 0, hook=mix_stat, residual=16)
            pe.wait_ge(root_ready, ST_MIX + 1)
            for j in range(1, GLU_PAIRS):
                pair(MIX_N + KC * j, MIX_G + j, j % 2)
            free(KV_G)
            for c in range(KC):
                unit(MIX_N + 16 + c, c, [0, 1, 2], KVR + ROPE, range(KC * c, KC * c + KC), xn, 0, DT - 1, [P, P, ROPE])
            free(ZQ_G)
            for c in range(KC):
                if c == 3:
                    stat(ST_KV, 0)
                unit(MIX_N + 20 + c, c, bank_set(1), 4 * P, range(KC * c, KC * c + KC), xn, 0, DT - 1)
            pe.wait_ge(root_ready, ST_KV + 1)
            pe.wait_ge(kv_lo, KVR // P)
            for h in range(2):
                pe.wait_ge(wlo_ready, MIX_N + 25 + h)
                for b in range(TB):
                    for k in range(KVR // P):
                        hi, lo = H[:, 16 + k, b * P:(b + 1) * P], H[:, 16 + k, TOK + b * P:TOK + (b + 1) * P]
                        whi, wlo = WHI[:, h, 512 * k:512 * k + 512], WLO[:, h, 512 * k:512 * k + 512]
                        out = PS[:, 2 * b + h, :]
                        mm(out, hi, whi, start=(k == 0), stop=False)
                        mm(out, hi, wlo, start=False, stop=False)
                        ins = mm(out, lo, whi, start=False, stop=(k == 1))
                ins.then_inc(units_used, 1)
            stat(ST_ZQ, 4)
            pe.wait_ge(root_ready, ST_ZQ + 1)
            for h in range(2):
                free(K_G + h)
                unit(MIX_N + 26 + h, h, bank_set(1 - h), 512, range(2), lambda k: H[:, 16 + k, :], 0, 1)
            pe.wait_ge(zq_lo, QR // P)
            for h in range(2):
                free(Q_G + h)
                unit(MIX_N + 28 + h, h, bank_set(1 - h), 512, range(KC), xn, 0, KC - 1)
            for h in range(2):
                free(R_G + h)
                unit(MIX_N + 30 + h, h, bank_set(1 - h, 2), 256, range(KC), xn, 0, KC - 1)

            pe.wait_ge(banks_free, Q_G + 1)
            pe.wait_ge(consts_loaded, 32)
            pe.wait_ge(kpe_sq, 1)
            for i in range(2):
                pe.wait_ge(hsq_ready, i + 1)
                for t in range(4):
                    ins = mm(PS[0:HEADS, 6, 0:TOK], SEL[:, 4 * i + t, :], (SQB, SUM[:])[i][:, t, :], start=(i + t == 0), stop=False)
                if i:
                    ins = mm(PS[0:HEADS, 6, 0:TOK], ONES[0:ROPE, 0:HEADS], KPSQ[:], start=False, stop=True)
                ins.then_inc(hstat_done, 1)
            for i in range(2, 5):
                pe.wait_ge(hsq_ready, i + 1)
                for t in range(4):
                    for b in range(TB):
                        lhs = (SQB, SUM[:])[i % 2][:, t, b * P:(b + 1) * P]
                        if i < 4:
                            at, rhs = 4 * (i - 2) + t + 8 * b, ONES[:, 0:1]
                        else:
                            at, rhs = 16 + 2 * t + 8 * b, HALVES
                        ins = mm(PS[:, 7, at:at + rhs.shape[1]], lhs, rhs, start=True, stop=True)
                ins.then_inc(hstat_done, 1)
            stat(ST_CONV, 5)
            pe.wait_ge(expand_loaded, 16)
            pe.wait_ge(krinv_ready, 1)
            pe.wait_ge(banks_free, R_G + 2)
            for j in range(HEADS // 2):
                for e in range(2):
                    h = 2 * j + e
                    ins = mm(PS[:, j, e * TOK:(e + 1) * TOK], EXPAND[:, h * P:(h + 1) * P], KRINV, start=True, stop=True)
                ins.then_inc(kbcast_done if j < HEADS // 2 - 1 else o_done, 1)
            pe.wait_ge(k_scaled, HEADS)
            pe.wait_ge(qrot_ready, 1)
            pe.wait_ge(qr_zeroed, 1)
            pe.wait_ge(o_lo_ready, 1)
            pe.wait_ge(root_ready, ST_CONV + 1)
            with pe.Fori(0, HEADS // 2) as i:
                for e in range(2):
                    pe.wait_ge(q_static, i * 2 + (e + 1))
                    pe.wait_ge(qr_static, i * 2 + (e + 1))
                    for b in range(TB):
                        out = PS[:, e, b * TOK:(b + 1) * TOK]
                        mm(out, QS[:, e, b * P:(b + 1) * P],
                           KN[:, ds(i * 2 + e, 1), :], start=True, stop=False)
                        ins = mm(out, QRS[e][:, b * P:(b + 1) * P], KRH[:, ds(i, 1), :], start=False, stop=True)
                    ins.then_inc(scores_done, 1)
                for e in range(2):
                    pe.wait_ge(probs_ready, i * 4 + (2 * e + 2))
                    for b in range(TB):
                        for k in range(TB):
                            ins = pe.transpose(PS[:, 2 + e, k * TOK + b * P:k * TOK + (b + 1) * P],
                                               PN[:, e, b, k * P:(k + 1) * P], IDENT[:])
                    ins.then_inc(probs_turned, 1)
                for e in range(2):
                    pe.wait_ge(probsT_ready, i * 2 + (e + 1))
                    pe.wait_ge(v_static, i * 2 + (e + 1))
                    pe.wait_ge(o_lo_ready, i * 2 + 1)
                    for k in range(TB):
                        ins = mm(PS[:, 4 + e, 0:TOK], VS[:, e, k, :], PT[e][:, k, :], start=(k == 0), stop=(k == 1))
                    ins.then_inc(o_done, 1)

            for m in range(4):
                g = WO_G + m
                if m == 0:
                    pe.wait_ge(o_lo_ready, HEADS + 1)
                free(g)
                for u, k0 in enumerate((8, 12, 0, 4)):
                    if u == 2:
                        pe.wait_ge(a_lo_ready, 1)
                    unit(WO_N + KC * m + u, u, bank_set(g % 2), 4 * P, range(k0, k0 + KC), hid, 8, 7)

            def ffn2_stat():
                pe.wait_ge(banks_free, FFN_G[1])
                stat(ST_FFN2, STAT_BANK[1])

            g = ffn(1, ffn2_stat, 32)
            turn_result(3, g)
            pe.wait_ge(sq_added, SQ_END[ST_OUT])
            for b in range(TB):
                for t in range(2):
                    ins = mm(PS[:, 3, b:b + 1], SQ[:, t, b * P:(b + 1) * P], ONES[:, 0:1], start=(t == 0), stop=(t == 1))
            ins.then_inc(stat_done, 1)


def kernel(**inputs):
    import concourse.bacc as bacc
    from concourse.bass_utils import run_bass_kernel_spmd

    nc = bacc.Bacc("TRN2", target_bir_lowering=False, num_devices=1)
    lane = np.arange(P)
    freq = (10000.0 ** (-(np.arange(ROPE // 2, dtype=np.float32) * 2.0 / ROPE))).astype(np.float32)
    consts = {
        "ident": np.eye(P, dtype=np.float32),
        "sel": np.ascontiguousarray(np.broadcast_to(np.eye(HEADS, dtype=np.float32), (P, HEADS, HEADS))),
        "expand": np.repeat(np.eye(HEADS, dtype=np.float32), P, axis=1),
        "freq": np.stack([freq[lane % 32], np.where(lane % 64 < 32, -1.0, 1.0), lane < ROPE, lane >= ROPE], 1).astype(np.float32),
    }
    arrays, io = {}, {}
    for name, a in {**inputs, **consts}.items():
        a = np.ascontiguousarray(a)
        arrays[f"in_{name}"] = a
        io[name] = nc.dram_tensor(f"in_{name}", a.shape, mybir.dt.from_np(a.dtype), kind="ExternalInput").ap()
    io["y"] = nc.dram_tensor("out_y", (1, TOK, DM), F32, kind="ExternalOutput").ap()
    build_layer(nc, io)
    return run_bass_kernel_spmd(nc, [arrays], core_ids=[0]).results[0]["out_y"]
```

```python
import concourse.bass as bass
import concourse.mybir as mybir
import numpy as np
from concourse.alu_op_type import AluOpType as ALU
from contextlib import ExitStack

F32, F32R, I32 = mybir.dt.float32, mybir.dt.float32r, mybir.dt.int32
ACT = mybir.ActivationFunctionType
AX = mybir.AxisListType
ds = bass.ds

P = 128
TOK = 256
TB = TOK // P
DM = 2048
DT = DM // P
FF = 5504
CONV = 1024
CT = CONV // P
TAPS = 31
PAD = TAPS // 2
HEADS, NOPE, ROPE, VD = 8, 128, 64, 128
QUAD = 4
QK = NOPE + ROPE
QR, KVR = 512, 256
EPS = 1e-6
SCALE = QK ** -0.5
KC = 4
UNIT = 2048
PARTS = [(0, 16), (16, 16), (32, 11)]
TWO_PI = 2 * np.pi
MAGIC = 1.5 * 2.0 ** 23


def pi_chunks():
    left, out = TWO_PI, []
    for grid in (2.0 ** -9, 2.0 ** -21, 2.0 ** -33, 2.0 ** -45):
        c = np.floor(left / grid) * grid
        out.append(float(c))
        left -= c
    return out


WEIGHTS = ["ffn1_w_gate", "ffn1_w_up", "ffn1_w_down", "w_in", "w_ukv", "w_uq", "w_out",
           "ffn2_w_gate", "ffn2_w_up", "ffn2_w_down"]

GAIN_ROWS = [("ffn1_norm", 16), ("mix_norm", 16), ("ffn2_norm", 16), ("final_norm", 16), ("conv_norm", 8),
             ("dw_bias", 8), ("q_norm", 4), ("kv_norm", 2)]
GAIN_AT, _r = {}, 0
for _n, _c in GAIN_ROWS:
    GAIN_AT[_n] = _r
    _r += _c
G_QN, G_KN, G_QR, G_KR = _r, _r + 1, _r + 2, _r + 3
GAINS = _r + 4

FULL_PAIRS = [n // 2 for _, n in PARTS]
PAIR_COUNT = [(n + 1) // 2 for _, n in PARTS]
DOWN_UNITS = [(n + KC - 1) // KC for _, n in PARTS]
PART_UNITS = [KC * PAIR_COUNT[i] + 4 * DOWN_UNITS[i] for i in range(3)]
PART_GROUPS = [PAIR_COUNT[i] + 4 for i in range(3)]
FFN_UNITS, FFN_GROUPS, FFN_PAIRS = sum(PART_UNITS), sum(PART_GROUPS), sum(PAIR_COUNT)
MIX_UNITS, MIX_GROUPS = 48, 21
GLU_PAIRS = CT // 2


def build_layer(nc, io):
    stack = ExitStack()
    with stack:
        def sb(name, shape, dt=F32):
            return stack.enter_context(nc.sbuf_tensor(name, shape, dt))

        def sem(name):
            return stack.enter_context(nc.semaphore(name))

        X = sb("X", [P, DT, TOK])
        with nc.sbuf_tensor("XF", [P, DT * 2 * TOK], F32) as XF:
            pass
        XN = sb("XN", [P, DT, 2 * TOK], F32R)
        H = sb("H", [P, 18, 2 * TOK], F32R)
        RAW = sb("RAW", [P, 2, UNIT])
        WHI = sb("WHI", [P, 2, UNIT], F32R)
        WLO = sb("WLO", [P, 2, UNIT], F32R)
        QWORK = sb("QWORK", [P, 4096])
        LOSUM = sb("LOSUM", [P, 4, TOK])
        SUM = sb("SUM", [P, 4, TOK])
        GATE = sb("GATE", [P, 2, TOK])
        HID = sb("HID", [P, 2, TOK])
        RINV = sb("RINV", [P, TOK])
        RINV2 = sb("RINV2", [P, TOK])
        ROOT = sb("ROOT", [P, TOK])
        SQ = sb("SQ", [P, 2, TOK])
        SQT = sb("SQT", [P, 2, TOK])
        U = sb("U", [P, CT, TOK + 2 * PAD])
        Y = sb("Y", [P, CT, TOK])
        KN = sb("KN", [P, HEADS, TOK])
        V = sb("V", [P, TB, HEADS * VD])
        KROT = sb("KROT", [P, TOK])
        KPSQ = sb("KPSQ", [ROPE, TOK])
        COS = sb("COS", [P, TOK])
        SIN = sb("SIN", [P, TOK])
        TAPW = sb("TAPW", [P, CT * TAPS])
        GAIN = sb("GAIN", [P, GAINS])
        IDENT = sb("IDENT", [P, P])
        ONES = sb("ONES", [P, P])
        SEL = sb("SEL", [P, HEADS, HEADS])
        EPST = sb("EPST", [P, 1])
        FREQ = sb("FREQ", [P, 4])
        QKG = sb("QKG", [P, 1])
        QSTAT = sb("QSTAT", [P, 4, 2 * HEADS])
        QRMS = sb("QRMS", [P, 2, 2 * HEADS])
        SMALL = sb("SMALL", [P, QUAD, 4, TB])

        PS = stack.enter_context(nc.psum_tensor("PS", [P, 8, 512], F32))

        QN = QWORK[:, 0:2048].rearrange("p (t n) -> p t n", t=8)
        QROT = QWORK[:, 2048:3072].rearrange("p (t n) -> p t n", t=4)
        SQB = QWORK[:, 3072:4096].rearrange("p (t n) -> p t n", t=4)
        PN = XF[:, 0:2048].rearrange("p (e b n) -> p e b n", e=QUAD, b=TB)
        KRH = XF[:, 2048:3072].rearrange("p (t n) -> p t n", t=4)
        QS = XF[:, 3072:4096].rearrange("p (e n) -> p e n", e=QUAD)
        VS = XF[:, 4096:5120].rearrange("p (e k n) -> p e k n", e=QUAD, k=TB)
        QRS = XF[:, 5120:6144].rearrange("p (e n) -> p e n", e=QUAD)
        PT = XF[:, 6144:8192].rearrange("p (e k n) -> p e k n", e=QUAD, k=TB)
        QG, QSW = (XF[:, a:a + 1024].rearrange("p (t n) -> p t n", t=4) for a in (6144, 7168))
        EXPAND = XF[0:HEADS, 3072:4096]
        PB = [LOSUM[:, 0:2, :], LOSUM[:, 2:4, :], SUM[:, 0:2, :], SUM[:, 2:4, :]]
        YG = QWORK[:, :].rearrange("p (t n) -> p t n", t=16)
        KG, KSW = GATE[:, 0, :], GATE[:, 1, :]
        KRINV = GATE[0:HEADS, 1, :]
        HALVES = FREQ[:, 2:4]
        TAB = Y

        x_loaded = [sem(f"x_loaded_{m}") for m in range(4)]
        sem_raw = [sem("raw_loaded_0"), sem("raw_loaded_1")]
        names = """whi_ready wlo_ready units_used banks_free losum_ready scaled gate_ready hid_ready
            h_hi_ready h_lo_ready x_updated x_hi_ready x_lo_ready sq_term sq_added stat_done root_ready rinv_ready
            ident_loaded consts_loaded gains_loaded taps_loaded pos_loaded expand_loaded ones_ready rope_step sin_ready trig_ready pads_ready glu_scaled sig_ready
            u_ready conv_dve conv_pool kv_scaled kv_normed kv_hi kv_lo kpe_gained kpe_moved kpe_mixed krot_ready kpe_sq
            zq_scaled zq_normed zq_hi zq_lo hsq_ready hstat_done kroot_ready krinv_ready kbcast_done
            k_scaled qstat_copied qstat_sum qroot_ready qrinv_ready qscale_ready qkg_ready qrot_gained qrot_moved
            qrot_mixed qrot_ready q_static v_static qr_static qr_zeroed scores_done max_ready bias_ready exp_ready den_ready
            probs_ready probs_turned probsT_ready o_done o_hi_ready o_lo_ready latent_sq y_scaled y_silu a_hi_ready
            a_lo_ready y_gained y_scaled_out stored""".split()
        S = {n: sem(n) for n in names}
        (whi_ready, wlo_ready, units_used, banks_free, losum_ready, scaled, gate_ready, hid_ready,
         h_hi_ready, h_lo_ready, x_updated, x_hi_ready, x_lo_ready, sq_term, sq_added, stat_done, root_ready,
         rinv_ready, ident_loaded, consts_loaded, gains_loaded, taps_loaded, pos_loaded, expand_loaded, ones_ready, rope_step, sin_ready, trig_ready, pads_ready,
         glu_scaled, sig_ready, u_ready, conv_dve, conv_pool, kv_scaled, kv_normed, kv_hi, kv_lo, kpe_gained, kpe_moved,
         kpe_mixed, krot_ready, kpe_sq, zq_scaled, zq_normed, zq_hi, zq_lo, hsq_ready, hstat_done,
         kroot_ready, krinv_ready, kbcast_done, k_scaled, qstat_copied, qstat_sum, qroot_ready, qrinv_ready,
         qscale_ready, qkg_ready, qrot_gained, qrot_moved, qrot_mixed, qrot_ready, q_static, v_static, qr_static, qr_zeroed,
         scores_done, max_ready, bias_ready, exp_ready, den_ready, probs_ready, probs_turned, probsT_ready, o_done,
         o_hi_ready, o_lo_ready, latent_sq, y_scaled, y_silu, a_hi_ready, a_lo_ready, y_gained, y_scaled_out,
         stored) = (S[n] for n in names)

        MIX_N, MIX_G, MIX_X = FFN_UNITS, FFN_GROUPS, 12
        FFN_N, FFN_G, FFN_X = [0, MIX_N + MIX_UNITS], [0, MIX_G + MIX_GROUPS], [0, MIX_X + 8]
        WO_N, WO_G = MIX_N + 32, MIX_G + 13
        KV_G, ZQ_G, V_G, K_G, R_G, Q_G = (MIX_G + i for i in (4, 5, 6, 7, 9, 11))
        ST_FFN1, ST_MIX, ST_KV, ST_ZQ, ST_CONV, ST_FFN2, ST_OUT = range(7)
        SQ_STEPS = [8, 8, 0, 0, 4, 8, 8]
        SQ_END = [sum(SQ_STEPS[:i + 1]) for i in range(7)]
        STAT_BANK = [4 - 4 * (g % 2) for g in FFN_G]

        CONV_STAT_M = 2
        CONV_STAT_BANK = 4 * ((WO_G + CONV_STAT_M + 1) % 2)
        OUT_BANK = 4 * ((FFN_G[1] + FFN_GROUPS) % 2)
        KBCAST_BANKS = [4, 5, 6, 0]
        ROPE_STEPS = 41

        def part_start(f, p):
            return (FFN_N[f] + sum(PART_UNITS[:p]), FFN_G[f] + sum(PART_GROUPS[:p]),
                    f * FFN_PAIRS + sum(PAIR_COUNT[:p]), FFN_X[f] + 4 * p)

        def over(r, n):
            return r.unsqueeze(1).broadcast_to([r.shape[0], n, TOK])

        def f32(a):
            return a.bitcast(F32)

        def gain(name, t):
            return GAIN[:, GAIN_AT[name] + t:GAIN_AT[name] + t + 1]

        def loads_by(n, c, uq_units):
            return n * 16 + (32 - 16 * (c % 2) + 32 * uq_units)

        CONV_DVE, CONV_POOL = [0, 2, 4, 5], [1, 3, 6, 7]
        DVE_STEPS, POOL_STEPS = TAPS + 1, 2 * TAPS - 1
        CONV_DVE_END, CONV_POOL_END = DVE_STEPS * len(CONV_DVE), POOL_STEPS * len(CONV_POOL)

        def half_of(w):
            return 1024 if w == 1536 else w // 2

        def window_of(t, k):
            return U[:, t, k:k + TOK], TAPW[:, t * TAPS + k:t * TAPS + k + 1]

        block = stack.enter_context(nc.Block())

        @block.sync
        def _(sp):
            slot_free_at = sp.alloc_register("slot_free_at")

            def load_x(m):
                sp.dma_start(X[:, 4 * m:4 * m + 4, :], io["x"][:, 4 * m:4 * m + 4, :]).then_inc(x_loaded[m], 16)

            def load(n, c, pieces):
                if not (isinstance(n, int) and n < 2):
                    free_at = n * 2 - 2
                    if not isinstance(n, int):
                        sp.reg_mov(slot_free_at, free_at)
                        free_at = slot_free_at
                        sp.wait_ge(wlo_ready, 1)
                    sp.wait_ge(wlo_ready, free_at)
                for dst, src in pieces:
                    sp.dma_start(dst, src).then_inc(sem_raw[c % 2], 16)
                if isinstance(n, int) and n == 0:
                    for m in range(1, 4):
                        load_x(m)

            def slot(c, kc, w):
                return RAW[:, c % 2, 0:kc * w].rearrange("p (k w) -> p k w", w=w)

            def load_two(n, c, k0, wa, ca, wb, cb, w):
                v = slot(c, KC, 2 * w)
                load(n, c, [(v[:, :, 0:w], wa[:, k0:k0 + KC, ds(ca, w)]),
                            (v[:, :, w:2 * w], wb[:, k0:k0 + KC, ds(cb, w)])])

            def load_one(n, c, k0, kc, wa, ca, w):
                v, h = slot(c, kc, w), kc // 2
                load(n, c, [(v[:, 0:h, :], wa[:, k0:k0 + h, ds(ca, w)]),
                            (v[:, h:kc, :], wa[:, k0 + h:k0 + kc, ds(ca, w)])])

            def rows(w):
                return w[0].rearrange("(k p) n -> p k n", p=P)

            def ffn(f):
                wg, wu, wd = (rows(io[f"ffn{f + 1}_w_{s}"]) for s in ("gate", "up", "down"))
                for p, (t0, nt) in enumerate(PARTS):
                    n, du = part_start(f, p)[0], DOWN_UNITS[p]

                    def pair(q, at, w=2 * P):
                        for c in range(KC):
                            col = q * (2 * P) + t0 * P
                            load_two(at + c, c, KC * c, wg, col, wu, col, w)

                    pair(0, n)
                    pair(1, n + KC)
                    with sp.Fori(1, FULL_PAIRS[p] // 2) as i:
                        for e in range(2):
                            pair(i * 2 + e, i * (2 * KC) + (n + e * KC))
                    for q in range(FULL_PAIRS[p] // 2 * 2, PAIR_COUNT[p]):
                        pair(q, n + KC * q, P * min(2, nt - 2 * q))
                    n += KC * PAIR_COUNT[p]
                    with sp.Fori(0, 2) as i:
                        for e in range(2):
                            for u in range(du):
                                c = e * du + u
                                load_one(i * (2 * du) + (n + c), c, t0 + KC * u, min(KC, nt - KC * u),
                                         wd, i * (8 * P) + e * 4 * P, 4 * P)

            load_x(0)
            ffn(0)
            w_in, w_out = rows(io["w_in"]), rows(io["w_out"])
            w_kv = io["w_ukv"][0].rearrange("(k p) (h s d) -> p k s h d", p=P, s=2, d=P)
            w_q = io["w_uq"][0].rearrange("(k p) (h d) -> p k h d", p=P, d=QK)
            for j in range(GLU_PAIRS):
                for c in range(KC):
                    load_two(MIX_N + 4 * j + c, c, KC * c, w_in, 2 * j * P, w_in, CONV + 2 * j * P, 2 * P)
            for c in range(KC):
                load_one(MIX_N + 16 + c, c, KC * c, KC, w_in, 2 * CONV + QR, KVR + ROPE)
            for c in range(KC):
                load_one(MIX_N + 20 + c, c, KC * c, KC, w_in, 2 * CONV, QR)
            for n, s in ((24, 1), (26, 0)):
                for c in range(2):
                    v = RAW[:, c, 0:1024].rearrange("p (k h d) -> p k h d", k=2, d=P)
                    load(MIX_N + n + c, c, [(v[:, k], w_kv[:, k, s, 4 * c:4 * c + 4]) for k in range(2)])
            for n, d0, d in ((28, NOPE, ROPE), (30, 0, NOPE)):
                for c in range(2):
                    v = RAW[:, c, 0:KC * 4 * d].rearrange("p (k h d) -> p k h d", k=KC, d=d)
                    load(MIX_N + n + c, c, [(v[:, k], w_q[:, k, 4 * c:4 * c + 4, d0:d0 + d]) for k in range(KC)])
            for n, k0 in ((WO_N, CT), (WO_N + 8, 0)):
                with sp.Fori(0, 2) as i:
                    for e in range(2):
                        for u in range(2):
                            load_one(i * 4 + (n + 2 * e + u), u, k0 + KC * u, KC, w_out, i * (8 * P) + e * 4 * P, 4 * P)
            ffn(1)
            for m in range(4):
                sp.wait_ge(y_scaled_out, m + 1)
                sp.dma_start(io["y"][:, 4 * m:4 * m + 4, :], YG[:, 4 * m:4 * m + 4, :]).then_inc(stored, 16)
            sp.wait_ge(stored, 16 * 4)

        @block.gpsimd
        def _(pool):
            done = {"term": 0, "added": 0}

            def square(a, first):
                if first:
                    pool.tensor_tensor(SQ[:], a, a, ALU.mult).then_inc(sq_added, 1)
                else:
                    pool.wait_ge(sq_added, done["added"])
                    pool.tensor_tensor(SQT[:], a, a, ALU.mult).then_inc(sq_term, 1)
                    done["term"] += 1
                    pool.wait_ge(sq_term, done["term"])
                    pool.tensor_tensor(SQ[:], SQ[:], SQT[:], ALU.add).then_inc(sq_added, 1)
                done["added"] += 1

            def residual_squares(m, update, st):
                if update is None:
                    pool.wait_ge(x_loaded[m], 16)
                else:
                    pool.wait_ge(x_updated, update + 1)
                for half in range(2):
                    if m == 0 and half == 0 and st > 0:
                        pool.wait_ge(stat_done, st)
                    t = 4 * m + 2 * half
                    square(X[:, t:t + 2, :], m == 0 and half == 0)

            pool.memset(ONES[:], 1.0).then_inc(ones_ready, 1)
            pool.memset(EPST[:], EPS).then_inc(ones_ready, 1)
            for m in range(4):
                residual_squares(m, None, ST_FFN1)

            pool.memset(U[:, :, 0:PAD], 0.0).then_inc(pads_ready, 1)
            pool.memset(U[:, :, PAD + TOK:], 0.0).then_inc(pads_ready, 1)

            def rotary_tables():
                steps = [0]

                def step(ins):
                    ins.then_inc(rope_step, 1)
                    steps[0] += 1
                    pool.wait_ge(rope_step, steps[0])

                chunk, A, K = pi_chunks(), TAB[:, 1, :], [TAB[:, 2, :], TAB[:, 3, :], TAB[:, 4, :]]
                pool.wait_ge(pos_loaded, 16)
                pool.wait_ge(consts_loaded, 32)
                step(pool.tensor_copy(A, TAB[:, 0, :].bitcast(I32)))
                step(pool.tensor_scalar(A, A, FREQ[:, 0:1], None, ALU.mult))

                def turns(k, scale):
                    step(pool.tensor_scalar(K[k], A, 1.0 / (TWO_PI * scale), MAGIC, ALU.mult, ALU.add))
                    step(pool.tensor_scalar(K[k], K[k], MAGIC, None, ALU.subtract))

                def take(k, c, scale):
                    step(pool.tensor_scalar(TAB[:, 6, :], K[k], chunk[c] * scale, None, ALU.mult))
                    step(pool.tensor_tensor(A, A, TAB[:, 6, :], ALU.subtract))

                big, mid = 2.0 ** 24, 2.0 ** 12
                turns(0, big)
                take(0, 0, big)
                take(0, 1, big)
                turns(1, mid)
                take(1, 0, mid)
                take(0, 2, big)
                take(1, 1, mid)
                turns(2, 1.0)
                for k, c, s in ((2, 0, 1.0), (1, 2, mid), (2, 1, 1.0), (0, 3, big), (1, 3, mid), (2, 2, 1.0), (2, 3, 1.0)):
                    take(k, c, s)
                turns(0, 1.0)
                for c in range(3):
                    take(0, c, 1.0)
                pi32 = 3.1415925
                pool.tensor_scalar(A, A, pi32, -pi32, ALU.min, ALU.max).then_inc(rope_step, 1)
                pool.wait_ge(sin_ready, 2)
                step_n = steps[0] + 1
                pool.tensor_scalar(SIN[:], SIN[:], FREQ[:, 1:2], None, ALU.mult).then_inc(trig_ready, 1)
                pool.tensor_tensor(COS[:], TAB[:, 5, :], TAB[:, 5, :], ALU.mult).then_inc(rope_step, 1)
                pool.wait_ge(rope_step, step_n + 1)
                pool.tensor_scalar(COS[:], COS[:], -2.0, 1.0, ALU.mult, ALU.add).then_inc(trig_ready, 1)

            def hidden_lo(q, tile, w=2):
                pool.wait_ge(h_hi_ready, q + 1)
                pool.tensor_tensor(H[:, ds(tile, w), TOK:], HID[:, 0:w, :], f32(H[:, ds(tile, w), 0:TOK]),
                                   ALU.subtract).then_inc(h_lo_ready, 1)

            def ffn(f):
                for p, (_, nt) in enumerate(PARTS):
                    _, _, q0, x0 = part_start(f, p)
                    with pool.Fori(0, FULL_PAIRS[p]) as i:
                        hidden_lo(i + q0, i * 2)
                    if nt % 2:
                        hidden_lo(q0 + FULL_PAIRS[p], nt - 1, 1)
                    if f == p == 0:
                        rotary_tables()
                for m in range(4):
                    residual_squares(m, x0 + m, (ST_MIX, ST_OUT)[f])

            ffn(0)

            order = [("mul", 0), ("mul", 1)]
            for k in range(1, TAPS - 1):
                order += [("mul", k + 1), ("add", k)]
            order.append(("add", TAPS - 1))
            step_of = {o: n + 1 for n, o in enumerate(order)}
            product = [SQT[:, 0, :], SQT[:, 1, :], HID[:, 1, :]]

            def conv(j, c):
                t, start = CONV_POOL[j], POOL_STEPS * j
                if c == 0:
                    pool.wait_ge(u_ready, t // 2 + 1)
                    pool.wait_ge(pads_ready, 2)
                    pool.wait_ge(taps_loaded, 16)
                    pool.wait_ge(sq_added, done["added"])
                for what, k in order[16 * c:16 * c + 16]:
                    if what == "mul":
                        u, tap = window_of(t, k)
                        if k == 0:
                            ins = pool.tensor_scalar(Y[:, t, :], u, tap, gain("dw_bias", t), ALU.mult, ALU.add)
                        else:
                            if k >= 4:
                                pool.wait_ge(conv_pool, start + step_of["add", k - 3])
                            elif j:
                                pool.wait_ge(conv_pool, start)
                            ins = pool.tensor_tensor(product[k % 3], u, tap.broadcast_to([P, TOK]), ALU.mult)
                    else:
                        pool.wait_ge(conv_pool, start + max(step_of["mul", k], step_of.get(("add", k - 1), 1)))
                        ins = pool.tensor_tensor(Y[:, t, :], Y[:, t, :], product[k % 3], ALU.add)
                    ins.then_inc(conv_pool, 1)

            for j in range(len(CONV_POOL) - 1):
                for c in range(4):
                    conv(j, c)
            pool.wait_ge(conv_dve, CONV_DVE_END)
            pool.wait_ge(conv_pool, POOL_STEPS * (len(CONV_POOL) - 1))
            pool.wait_ge(stat_done, ST_CONV)
            for t in range(0, CT - 2, 2):
                square(Y[:, t:t + 2, :], t == 0)
            for c in range(4):
                conv(len(CONV_POOL) - 1, c)
            pool.wait_ge(conv_pool, CONV_POOL_END)
            square(Y[:, CT - 2:, :], False)
            for m in range(4):
                residual_squares(m, MIX_X + 4 + m, ST_FFN2)
            ffn(1)

        @block.scalar
        def _(act):
            uq_units = [0]
            half_in = [UNIT // 2, UNIT // 2]

            def split(n, c, w=UNIT):
                act.wait_ge(sem_raw[c % 2], loads_by(n, c, uq_units[0]))
                for h, (a, b) in enumerate(((0, half_of(w)), (half_of(w), w))):
                    if not (isinstance(n, int) and n < 2):
                        whole = h or b > half_in[c % 2]
                        act.wait_ge(units_used, n * 2 - (2 if whole else 3))
                    act.activation(WHI[:, c % 2, a:b], RAW[:, c % 2, a:b], ACT.Copy).then_inc(whi_ready, 1)
                half_in[c % 2] = half_of(w)

            def losum(g, s, used, nt=4):
                act.wait_ge(units_used, used * 2)
                if not (isinstance(g, int) and g < 1):
                    act.wait_ge(banks_free, g)
                act.activation(LOSUM[:, 0:nt, :], PS[:, 4 * s:4 * s + nt, TOK:], ACT.Copy).then_inc(losum_ready, 1)

            def silu(q, w=2):
                act.wait_ge(scaled, q + 1)
                act.activation(GATE[:, 0:w, :], SUM[:, 0:w, :], ACT.Silu).then_inc(gate_ready, 1)

            def hidden_hi(q, tile, w=2):
                act.wait_ge(hid_ready, q + 1)
                act.activation(H[:, ds(tile, w), 0:TOK], HID[:, 0:w, :], ACT.Copy).then_inc(h_hi_ready, 1)

            def residual_hi(m, update, name, idx):
                if update is None:
                    act.wait_ge(x_loaded[m], 16)
                else:
                    act.wait_ge(x_updated, update + 1)
                for t in range(4 * m, 4 * m + 4):
                    act.activation(XN[:, t, 0:TOK], X[:, t, :], ACT.Copy, scale=gain(name, t)).then_inc(x_hi_ready, 1)

            def root(st, src, dst, scale, also=None):
                act.wait_ge(stat_done, st + 1)
                if st:
                    act.wait_ge(rinv_ready, st)
                act.activation(dst, src, ACT.Sqrt, scale=scale, bias=EPST[:, 0:1]).then_inc(root_ready, 1)

            def no():
                pass

            act.dma_start(GAIN[:], io["gains"]).then_inc(gains_loaded, 16)
            act.dma_start(IDENT[:], io["ident"]).then_inc(ident_loaded, 16)
            act.dma_start(SEL[:], io["sel"]).then_inc(consts_loaded, 16)
            act.dma_start(FREQ[:], io["freq"]).then_inc(consts_loaded, 16)
            act.dma_start(TAPW[:], io["taps"]).then_inc(taps_loaded, 16)
            act.dma_start(TAB[:, 0, :].bitcast(I32),
                          io["positions"][0].partition_broadcast(P)).then_inc(pos_loaded, 16)
            act.wait_ge(gains_loaded, 16)
            for m in range(4):
                residual_hi(m, None, "ffn1_norm", m)
                if m < 2:
                    split(m, m)

            def first_root():
                root(ST_FFN1, PS[:, STAT_BANK[0], 0:TOK], ROOT[:], 1.0 / DM)

            def sines():
                act.wait_ge(rope_step, ROPE_STEPS)
                act.activation(SIN[:], TAB[:, 1, :], ACT.Sin).then_inc(sin_ready, 1)
                act.activation(TAB[:, 5, :], TAB[:, 1, :], ACT.Sin, scale=0.5).then_inc(sin_ready, 1)

            def window(n, jobs, w=UNIT, count=KC, skip=0):
                for c in range(skip, count):
                    split(n + c, c, w)
                    if 0 < c <= len(jobs):
                        jobs[c - 1]()

            def ffn(f, before, extra):
                for p, (_, nt) in enumerate(PARTS):
                    n, g, q0, x0 = part_start(f, p)
                    du = DOWN_UNITS[p]

                    def pair_jobs(q, g, s, used, tile, w=2):
                        return [lambda: losum(g, s, used, 2 * w), lambda: silu(q, w), lambda: hidden_hi(q, tile, w)]

                    if f == p == 0:
                        window(n, [], skip=2)
                        extra()
                    else:
                        window(n, before + [extra if p == 0 else no])
                    s0 = g % 2
                    window(n + KC, pair_jobs(q0, g, s0, n + KC, 0))
                    if (f, p) == (0, 1):
                        sines()
                    with act.Fori(1, FULL_PAIRS[p] // 2) as i:
                        for e in range(2):
                            window(i * (2 * KC) + (n + KC * e),
                                   pair_jobs(i * 2 + (q0 + e - 1), i * 2 + (g + e - 1), (s0 + e + 1) % 2,
                                             i * (2 * KC) + (n + KC * e), i * 4 + (2 * e - 2)))
                    for q in range(FULL_PAIRS[p] // 2 * 2, PAIR_COUNT[p]):
                        window(n + KC * q, pair_jobs(q0 + q - 1, g + q - 1, (s0 + q + 1) % 2, n + KC * q, 2 * q - 2),
                               KC * 2 * P * min(2, nt - 2 * q))
                    n, g = n + KC * PAIR_COUNT[p], g + PAIR_COUNT[p]
                    last = nt - 2 * (PAIR_COUNT[p] - 1)
                    jobs = pair_jobs(q0 + PAIR_COUNT[p] - 1, g - 1, (g - 1) % 2, n, nt - last, last)
                    for m in range(4):
                        for u in range(du):
                            split(n + du * m + u, du * m + u, 4 * P * min(KC, nt - KC * u))
                            if u:
                                jobs[u - 1]()
                        if du == 3 and len(jobs) > 2:
                            jobs[2]()
                        jobs = [lambda m=m, g=g, n=n, du=du: losum(g + m, (g + m) % 2, n + du * (m + 1)), no, no]
                        if p == 2 and f == 0:
                            jobs[1] = lambda m=m, x0=x0: residual_hi(m, x0 + m, "mix_norm", 4 + m)
                        if p == 2 and f == 1:
                            jobs[1] = lambda m=m, x0=x0: final_gain(m, x0 + m)
                    before = jobs[0:2]
                return jobs

            def final_gain(m, update):
                act.wait_ge(x_updated, update + 1)
                for t in range(4 * m, 4 * m + 4):
                    act.activation(YG[:, t, :], X[:, t, :], ACT.Copy, scale=gain("final_norm", t)).then_inc(y_gained, 1)

            jobs = ffn(0, [], first_root)

            def glu_jobs(j):
                def sigmoid():
                    act.wait_ge(glu_scaled, j + 1)
                    act.activation(GATE[:], SUM[:, 2:4, :], ACT.Sigmoid).then_inc(sig_ready, 1)
                return [lambda: losum(MIX_G + j, j % 2, MIX_N + KC * (j + 1)), sigmoid]

            window(MIX_N, [jobs[0], jobs[1], lambda: root(ST_MIX, PS[:, 4, 0:TOK], ROOT[:], 1.0 / DM)])
            for j in range(1, GLU_PAIRS):
                window(MIX_N + KC * j, glu_jobs(j - 1))
            window(MIX_N + 16, glu_jobs(GLU_PAIRS - 1), KC * (KVR + ROPE))

            def kv_losum():
                act.wait_ge(units_used, 2 * (MIX_N + 20))
                act.wait_ge(banks_free, KV_G)
                act.activation(LOSUM[:, 0:2, :], PS[:, 0:2, TOK:], ACT.Copy).then_inc(losum_ready, 1)
                act.activation(LOSUM[0:ROPE, 2, :], PS[0:ROPE, 2, TOK:], ACT.Copy).then_inc(losum_ready, 1)

            def kpe_moves():
                act.wait_ge(kpe_gained, 1)
                h = ROPE // 2
                for dst, d0, s0, n in ((KG, ROPE, 0, ROPE), (KSW, 0, h, h), (KSW, h, 0, h),
                                       (KSW, ROPE, h, h), (KSW, ROPE + h, 0, h)):
                    act.activation(dst[d0:d0 + n, :], KG[s0:s0 + n, :], ACT.Copy).then_inc(kpe_moved, 1)

            def latent_hi(count, ready, n, dst, name):
                act.wait_ge(ready, 1)
                for t in range(n):
                    act.activation(dst[:, t, 0:TOK], SUM[:, t, :], ACT.Copy, scale=gain(name, t)).then_inc(count, 1)

            split(MIX_N + 20, 0)
            split(MIX_N + 21, 1)
            kv_losum()
            split(MIX_N + 22, 0)
            act.wait_ge(kv_scaled, 1)
            act.activation(SQB[:, 0:2, :], SUM[:, 0:2, :], ACT.Square).then_inc(latent_sq, 1)
            act.activation(KPSQ[:], SUM[0:ROPE, 2, :], ACT.Square).then_inc(kpe_sq, 1)
            kpe_moves()
            split(MIX_N + 23, 1)
            root(ST_KV, PS[:, 0, 0:TOK], ROOT[:], 1.0 / KVR)
            latent_hi(kv_hi, kv_normed, KVR // P, H[:, 16:18], "kv_norm")
            split(MIX_N + 24, 0, 1024)
            losum(ZQ_G, 1, MIX_N + 24)
            split(MIX_N + 25, 1, 1024)
            act.wait_ge(zq_scaled, 1)
            act.wait_ge(stat_done, ST_KV + 1)
            act.activation(SQB, SUM[:], ACT.Square).then_inc(latent_sq, 1)
            split(MIX_N + 26, 0, 1024)
            root(ST_ZQ, PS[:, 4, 0:TOK], ROOT[:], 1.0 / QR)
            act.wait_ge(units_used, 2 * (MIX_N + 26))
            act.wait_ge(banks_free, V_G)
            act.activation(V[:, :, :].rearrange("p b (h n) -> p (b h) n", n=512), PS[:, 0:4, :],
                           ACT.Copy).then_inc(banks_free, 1)
            split(MIX_N + 27, 1, 1024)
            latent_hi(zq_hi, zq_normed, QR // P, XN, "q_norm")
            losum(K_G, 1, MIX_N + 27)
            uq_units[0] = 1
            split(MIX_N + 28, 0, 1024)
            act.dma_start(EXPAND, io["expand"]).then_inc(expand_loaded, 16)
            losum(K_G + 1, 0, MIX_N + 28)
            split(MIX_N + 29, 1, 1024)

            SQ_OF = ((KN[:, 0:4], K_G), (KN[:, 4:8], K_G + 1), (QROT, R_G + 1), (QN[:, 0:4], Q_G), (QN[:, 4:8], Q_G + 1))

            def head_squares(i):
                src, group = SQ_OF[i]
                act.wait_ge(banks_free, group + 1)
                if i >= 2:
                    act.wait_ge(hstat_done, i - 1)
                act.activation((SQB, SUM[:])[i % 2], src, ACT.Square).then_inc(hsq_ready, 1)

            head_squares(0)
            losum(R_G, 1, MIX_N + 29, 2)
            head_squares(1)
            uq_units[0] = 2
            split(MIX_N + 30, 0)
            losum(R_G + 1, 0, MIX_N + 30, 2)
            split(MIX_N + 31, 1)
            act.wait_ge(hstat_done, 2)
            act.activation(ROOT[0:HEADS, :], PS[0:HEADS, 2, 0:TOK], ACT.Sqrt, scale=1.0 / QK,
                           bias=EPST[0:HEADS, 0:1]).then_inc(kroot_ready, 1)
            act.wait_ge(banks_free, R_G + 2)
            act.activation(QG, QROT, ACT.Copy, scale=GAIN[:, G_QR:G_QR + 1]).then_inc(qrot_gained, 1)
            head_squares(2)
            losum(Q_G, 1, MIX_N + 31)
            split(MIX_N + 32, 0)
            act.wait_ge(qrot_gained, 1)
            h = ROPE // 2
            for d in range(4):
                src = d ^ 1
                act.activation(QSW[d * h:(d + 1) * h], QG[src * h:(src + 1) * h], ACT.Copy).then_inc(qrot_moved, 1)
            head_squares(3)
            losum(Q_G + 1, 0, MIX_N + 32)
            split(MIX_N + 33, 1)
            head_squares(4)
            act.wait_ge(hstat_done, 5)
            act.activation(QSTAT[:, 0, :], PS[:, 7, 16:32], ACT.Copy).then_inc(qstat_copied, 1)
            act.wait_ge(qstat_sum, 1)
            act.activation(QSTAT[:, 2, :], QSTAT[:, 1, :], ACT.Sqrt, scale=1.0 / QK,
                           bias=EPST[:, 0:1]).then_inc(qroot_ready, 1)
            act.wait_ge(qkg_ready, 1)
            with act.Fori(0, HEADS // QUAD) as i:
                for e in range(QUAD):
                    act.wait_ge(o_done, i * QUAD + 1)
                    act.activation(QS[:, e, :], QN[:, ds(i * QUAD + e, 1), :], ACT.Copy,
                                   scale=QKG[:, 0:1]).then_inc(q_static, 1)
                    r = slice(e % 2 * ROPE, (e % 2 + 1) * ROPE)
                    act.activation(QRS[r, e, :].unsqueeze(1), QROT[r, ds(i * 2 + e // 2, 1), :],
                                   ACT.Copy).then_inc(qr_static, 1)
                for e in range(QUAD):
                    act.wait_ge(bias_ready, i * QUAD + (e + 1))
                    for b in range(TB):
                        act.activation(PB[e][:, b, :], PS[:, e, b * TOK:(b + 1) * TOK], ACT.Exp,
                                       bias=SMALL[:, e, 1, b:b + 1], scale=QRMS[:, 1, ds(i * QUAD + (e + 8 * b), 1)],
                                       accum_out=SMALL[:, e, 2, b:b + 1]).then_inc(exp_ready, 1)
                for e in range(QUAD):
                    act.wait_ge(probs_turned, i * QUAD + (e + 1))
                    act.activation(PT[:, e, :, :].rearrange("p k n -> p (k n)"), PS[:, 4 + e, :],
                                   ACT.Copy).then_inc(probsT_ready, 1)
                for e in range(QUAD):
                    act.wait_ge(o_done, i * QUAD + (e + 2))
                    act.activation(H[:, ds(i * QUAD + (8 + e), 1), 0:TOK], PS[:, e, 0:TOK],
                                   ACT.Copy).then_inc(o_hi_ready, 1)

            def swish():
                for t in range(CT):
                    act.wait_ge(y_scaled, t // 4 + 1)
                    act.activation(Y[:, t, :], Y[:, t, :], ACT.Silu, scale=gain("conv_norm", t)).then_inc(y_silu, 1)

            def swish_hi():
                for t in (0, 4):
                    act.wait_ge(y_silu, t + 4)
                    act.activation(H[:, t:t + 4, 0:TOK], Y[:, t:t + 4, :], ACT.Copy).then_inc(a_hi_ready, 1)

            jobs = []
            for m in range(8):
                n, g = WO_N + 2 * m, WO_G + m
                for u in range(2):
                    if m:
                        split(n + u, u)
                    if jobs:
                        jobs.pop(0)()
                jobs = [lambda g=g, n=n: losum(g, g % 2, n + 2), lambda: None]
                if m == CONV_STAT_M:
                    late = jobs[0]
                    jobs = [lambda: (root(ST_CONV, PS[:, CONV_STAT_BANK, 0:TOK], ROOT[:], 1.0 / CONV), late()),
                            lambda: (swish(), swish_hi())]
                if m >= 4:
                    jobs[1] = lambda m=m: residual_hi(m - 4, MIX_X + m, "ffn2_norm", 4 + m)
            jobs = ffn(1, jobs, lambda: root(ST_FFN2, PS[:, STAT_BANK[1], 0:TOK], ROOT[:], 1.0 / DM))
            for job in jobs:
                job()
            root(ST_OUT, PS[:, OUT_BANK, 0:TOK], ROOT[:], 1.0 / DM)

        @block.vector
        def _(dve):
            def split(n, c, w=UNIT):
                for h, (a, b) in enumerate(((0, half_of(w)), (half_of(w), w))):
                    dve.wait_ge(whi_ready, n * 2 + (h + 1))
                    dve.tensor_tensor(WLO[:, c % 2, a:b], RAW[:, c % 2, a:b], f32(WHI[:, c % 2, a:b]),
                                      ALU.subtract).then_inc(wlo_ready, 1)

            def window(n, jobs, w=UNIT, skip=0):
                for c in range(skip, KC):
                    split(n + c, c, w)
                    if 0 < c <= len(jobs):
                        jobs[c - 1]()

            def no():
                pass

            def add_halves(g, s, nt, dst, count=None):
                dve.wait_ge(losum_ready, g + 1 if count is None else count)
                dve.tensor_tensor(dst, PS[:, 4 * s:4 * s + nt, 0:TOK], LOSUM[:, 0:nt, :], ALU.add).then_inc(banks_free, 1)

            def pair_sums(q, g, s, stat, w=2):
                add_halves(g, s, 2 * w, SUM[:, 0:2 * w, :])
                dve.wait_ge(banks_free, g + 1)
                dve.wait_ge(rinv_ready, stat + 1)
                dve.tensor_tensor(SUM[:, 0:2 * w, :], SUM[:, 0:2 * w, :], over(RINV[:], 2 * w), ALU.mult).then_inc(scaled, 1)

            def hidden(q, w=2):
                dve.wait_ge(gate_ready, q + 1)
                if not (isinstance(q, int) and q < 1):
                    dve.wait_ge(h_lo_ready, q)
                dve.tensor_tensor(HID[:, 0:w, :], GATE[:, 0:w, :], SUM[:, w:2 * w, :], ALU.mult).then_inc(hid_ready, 1)

            def residual_add(g, m, scale):
                add_halves(g, g % 2, 4, SUM[:])
                dve.wait_ge(banks_free, g + 1)
                xs = X[:, 4 * m:4 * m + 4, :]
                dve.scalar_tensor_tensor(out=xs, in0=SUM[:], scalar=scale, in1=xs,
                                         op0=ALU.mult, op1=ALU.add).then_inc(x_updated, 1)

            def residual_lo(m, name, idx):
                for t in range(4):
                    k = 4 * m + t
                    dve.wait_ge(x_hi_ready, 4 * idx + t + 1)
                    dve.scalar_tensor_tensor(out=XN[:, k, TOK:], in0=X[:, k, :], scalar=gain(name, k),
                                             in1=f32(XN[:, k, 0:TOK]), op0=ALU.mult,
                                             op1=ALU.subtract).then_inc(x_lo_ready, 1)

            def inverse(st, dst):
                dve.wait_ge(root_ready, st + 1)
                dve.reciprocal(dst, ROOT[:]).then_inc(rinv_ready, 1)

            def ffn(f, before, stat):
                for p, (_, nt) in enumerate(PARTS):
                    n, g, q0, x0 = part_start(f, p)
                    du, s0 = DOWN_UNITS[p], g % 2

                    def pair_jobs(q, g, s, w=2):
                        return [lambda: pair_sums(q, g, s, stat, w), lambda: hidden(q, w)]

                    if f == p == 0:
                        window(n, [], skip=2)
                        inverse(stat, RINV[:])
                    else:
                        window(n, before + [lambda: inverse(stat, RINV[:]) if p == 0 else no()])
                    window(n + KC, pair_jobs(q0, g, s0))
                    with dve.Fori(1, FULL_PAIRS[p] // 2) as i:
                        for e in range(2):
                            window(i * (2 * KC) + (n + KC * e),
                                   pair_jobs(i * 2 + (q0 + e - 1), i * 2 + (g + e - 1), (s0 + e + 1) % 2))
                    for q in range(FULL_PAIRS[p] // 2 * 2, PAIR_COUNT[p]):
                        window(n + KC * q, pair_jobs(q0 + q - 1, g + q - 1, (s0 + q + 1) % 2),
                               KC * 2 * P * min(2, nt - 2 * q))
                    n, g = n + KC * PAIR_COUNT[p], g + PAIR_COUNT[p]
                    last = nt - 2 * (PAIR_COUNT[p] - 1)
                    jobs = pair_jobs(q0 + PAIR_COUNT[p] - 1, g - 1, (g - 1) % 2, last)
                    for m in range(4):
                        for u in range(du):
                            split(n + du * m + u, du * m + u, 4 * P * min(KC, nt - KC * u))
                            if 0 < u <= len(jobs):
                                jobs[u - 1]()
                        jobs = [lambda m=m, g=g: residual_add(g + m, m, 0.5), no]
                        if p == 2 and f == 0:
                            jobs[1] = lambda m=m: residual_lo(m, "mix_norm", 4 + m)
                    before = jobs
                return jobs

            for m in range(4):
                dve.wait_ge(x_loaded[m], 16)
                dve.wait_ge(gains_loaded, 16)
                residual_lo(m, "ffn1_norm", m)
                if m < 2:
                    split(m, m)
            dve.tensor_tensor(QKG[:], GAIN[:, G_QN:G_QN + 1], GAIN[:, G_KN:G_KN + 1], ALU.mult).then_inc(qkg_ready, 1)
            jobs = ffn(0, [], ST_FFN1)

            def conv(j, c):
                t, start, acc2 = CONV_DVE[j], DVE_STEPS * j, HID[:, 0, :]
                if c == 0:
                    dve.wait_ge(u_ready, t // 2 + 1)
                    dve.wait_ge(pads_ready, 2)
                    dve.wait_ge(taps_loaded, 16)
                for k in range(8 * c, 8 * c + 8):
                    acc = acc2 if k % 2 else Y[:, t, :]
                    if k == TAPS:
                        dve.wait_ge(conv_dve, start + k)
                        ins = dve.tensor_tensor(Y[:, t, :], Y[:, t, :], acc2, ALU.add)
                    elif k == 0:
                        u, tap = window_of(t, k)
                        ins = dve.tensor_scalar(acc, u, tap, gain("dw_bias", t), ALU.mult, ALU.add)
                    elif k == 1:
                        if j:
                            dve.wait_ge(conv_dve, start)
                        u, tap = window_of(t, k)
                        ins = dve.tensor_scalar(acc, u, tap, None, ALU.mult)
                    else:
                        u, tap = window_of(t, k)
                        dve.wait_ge(conv_dve, start + k - 1)
                        ins = dve.scalar_tensor_tensor(out=acc, in0=u, scalar=tap, in1=acc, op0=ALU.mult, op1=ALU.add)
                    ins.then_inc(conv_dve, 1)

            def glu_sums(j):
                if j:
                    dve.wait_ge(u_ready, j)
                add_halves(MIX_G + j, j % 2, 4, SUM[:])
                dve.wait_ge(banks_free, MIX_G + j + 1)
                dve.wait_ge(rinv_ready, ST_MIX + 1)
                dve.tensor_tensor(SUM[:], SUM[:], over(RINV[:], 4), ALU.mult).then_inc(glu_scaled, 1)

            def glu(j):
                dve.wait_ge(sig_ready, j + 1)
                dve.tensor_tensor(U[:, 2 * j:2 * j + 2, PAD:PAD + TOK], SUM[:, 0:2, :], GATE[:],
                                  ALU.mult).then_inc(u_ready, 1)

            def scale_by(dst, r, count):
                dve.tensor_tensor(dst, dst, r, ALU.mult).then_inc(count, 1)

            window(MIX_N, jobs + [lambda: inverse(ST_MIX, RINV[:])])
            quarters = [(j, c) for j in range(2) for c in range(4)]
            for j in range(1, GLU_PAIRS + 1):
                for c in range(KC):
                    split(MIX_N + KC * j + c, c, UNIT if j < GLU_PAIRS else KC * (KVR + ROPE))
                    if c == 1:
                        glu_sums(j - 1)
                    if j >= 2 and c != 1 and len(quarters):
                        conv(*quarters.pop(0))
                    if c == 2:
                        glu(j - 1)
            split(MIX_N + 20, 0)
            conv(2, 0)
            split(MIX_N + 21, 1)
            dve.wait_ge(u_ready, GLU_PAIRS)
            dve.wait_ge(losum_ready, KV_G + 2)
            dve.tensor_tensor(SUM[:, 0:2, :], PS[:, 0:2, 0:TOK], LOSUM[:, 0:2, :], ALU.add)
            dve.tensor_tensor(SUM[0:ROPE, 2, :], PS[0:ROPE, 2, 0:TOK], LOSUM[0:ROPE, 2, :], ALU.add).then_inc(banks_free, 1)
            dve.wait_ge(banks_free, KV_G + 1)
            dve.tensor_tensor(SUM[:, 0:2, :], SUM[:, 0:2, :], over(RINV[:], 2), ALU.mult)
            scale_by(SUM[0:ROPE, 2, :], RINV[0:ROPE, :], kv_scaled)
            dve.wait_ge(kv_scaled, 1)
            dve.tensor_scalar(KG[0:ROPE, :], SUM[0:ROPE, 2, :], GAIN[0:ROPE, G_KR:G_KR + 1], None,
                              ALU.mult).then_inc(kpe_gained, 1)
            conv(2, 1)
            split(MIX_N + 22, 0)
            conv(2, 2)
            split(MIX_N + 23, 1)
            inverse(ST_KV, RINV2[:])
            dve.wait_ge(rinv_ready, ST_KV + 1)
            scale_by(SUM[:, 0:2, :], over(RINV2[:], 2), kv_normed)
            dve.wait_ge(kpe_moved, 5)
            dve.wait_ge(trig_ready, 2)
            dve.tensor_tensor(KROT[:], KG, COS[:], ALU.mult).then_inc(kpe_mixed, 1)
            scale_by(KSW, SIN[:], kpe_mixed)

            def latent_lo(count, hi, normed, n, dst, name):
                dve.wait_ge(normed, 1)
                for t in range(n):
                    dve.wait_ge(hi, t + 1)
                    dve.scalar_tensor_tensor(out=dst[:, t, TOK:], in0=SUM[:, t, :], scalar=gain(name, t),
                                             in1=f32(dst[:, t, 0:TOK]), op0=ALU.mult, op1=ALU.subtract).then_inc(count, 1)

            latent_lo(kv_lo, kv_hi, kv_normed, KVR // P, H[:, 16:18], "kv_norm")
            dve.wait_ge(kpe_mixed, 2)
            dve.tensor_tensor(KROT[:], KROT[:], KSW, ALU.add).then_inc(krot_ready, 1)
            split(MIX_N + 24, 0, 1024)
            dve.wait_ge(kpe_sq, 1)
            dve.wait_ge(kv_lo, KVR // P)
            add_halves(ZQ_G, 1, 4, SUM[:], ZQ_G + 2)
            dve.wait_ge(banks_free, ZQ_G + 1)
            scale_by(SUM[:], over(RINV[:], 4), zq_scaled)
            split(MIX_N + 25, 1, 1024)
            conv(2, 3)
            split(MIX_N + 26, 0, 1024)
            inverse(ST_ZQ, RINV2[:])
            dve.wait_ge(rinv_ready, ST_ZQ + 1)
            scale_by(SUM[:], over(RINV2[:], 4), zq_normed)
            split(MIX_N + 27, 1, 1024)
            latent_lo(zq_lo, zq_hi, zq_normed, QR // P, XN, "q_norm")
            add_halves(K_G, 1, 4, KN[:, 0:4, :])
            split(MIX_N + 28, 0, 1024)
            add_halves(K_G + 1, 0, 4, KN[:, 4:8, :])
            split(MIX_N + 29, 1, 1024)
            conv(3, 0)
            add_halves(R_G, 1, 2, QROT[:, 0:2, :])
            split(MIX_N + 30, 0)
            add_halves(R_G + 1, 0, 2, QROT[:, 2:4, :])
            split(MIX_N + 31, 1)
            conv(3, 1)
            halves = QRS.rearrange("p (t e) n -> p t e n", e=2)
            dve.memset(halves[ROPE:, :, 0, :], 0.0).then_inc(qr_zeroed, 1)
            dve.memset(halves[0:ROPE, :, 1, :], 0.0).then_inc(o_lo_ready, 1)
            dve.wait_ge(kroot_ready, 1)
            dve.wait_ge(krot_ready, 1)
            dve.reciprocal(KRINV, ROOT[0:HEADS, :]).then_inc(krinv_ready, 1)
            add_halves(Q_G, 1, 4, QN[:, 0:4, :])
            split(MIX_N + 32, 0)
            conv(3, 2)
            dve.wait_ge(qrot_moved, 4)
            dve.wait_ge(hsq_ready, 3)
            dve.tensor_tensor(QROT, QG, over(COS[:], 4), ALU.mult).then_inc(qrot_mixed, 1)
            scale_by(QSW, over(SIN[:], 4), qrot_mixed)
            dve.wait_ge(qrot_mixed, 2)
            dve.tensor_tensor(QROT, QROT, QSW, ALU.add).then_inc(qrot_ready, 1)
            add_halves(Q_G + 1, 0, 4, QN[:, 4:8, :])
            split(MIX_N + 33, 1)
            for j in range(HEADS // 2):
                if j < HEADS // 2 - 1:
                    dve.wait_ge(kbcast_done, j + 1)
                else:
                    dve.wait_ge(o_done, 1)
                dve.tensor_tensor(KN[:, 2 * j:2 * j + 2, :], KN[:, 2 * j:2 * j + 2, :],
                                  PS[:, KBCAST_BANKS[j], :].rearrange("p (e n) -> p e n", e=2), ALU.mult)
                for e in range(2):
                    r = slice(e * ROPE, (e + 1) * ROPE)
                    dve.tensor_tensor(KRH[r, j, :], KROT[r, :], PS[r, KBCAST_BANKS[j], e * TOK:(e + 1) * TOK],
                                      ALU.mult).then_inc(k_scaled, 1)
            conv(3, 3)
            dve.wait_ge(qstat_copied, 1)
            dve.tensor_tensor(QSTAT[:, 1, :], PS[:, 7, 0:16], QSTAT[:, 0, :], ALU.add).then_inc(qstat_sum, 1)
            dve.wait_ge(qroot_ready, 1)
            dve.reciprocal(QRMS[:, 0, :], QSTAT[:, 2, :]).then_inc(qrinv_ready, 1)
            dve.wait_ge(qrinv_ready, 1)
            dve.tensor_scalar(QRMS[:, 1, :], QRMS[:, 0, :], SCALE, None, ALU.mult).then_inc(qscale_ready, 1)
            dve.tensor_scalar(QSTAT[:, 3, :], QRMS[:, 0, :], -SCALE, None, ALU.mult).then_inc(qscale_ready, 1)
            dve.wait_ge(banks_free, V_G + 1)
            with dve.Fori(0, HEADS // QUAD) as i:
                dve.wait_ge(o_done, i * QUAD + 1)
                for e in range(QUAD):
                    dve.tensor_copy(VS[:, e, :, :], V[:, :, ds(i * (QUAD * VD) + e * VD, VD)]).then_inc(v_static, 1)
                for e in range(QUAD):
                    dve.wait_ge(scores_done, i * QUAD + (e + 1))
                    dve.reduce_max(SMALL[:, e, 0, :], PS[:, e, :].rearrange("p (b n) -> p b n", b=TB),
                                   AX.X).then_inc(max_ready, 1)
                    dve.wait_ge(max_ready, i * QUAD + (e + 1))
                    dve.tensor_tensor(SMALL[:, e, 1, :].unsqueeze(2), SMALL[:, e, 0, :].unsqueeze(2),
                                      QSTAT[:, 3, :].rearrange("p (b h) -> p b h", b=TB)[:, :, ds(i * QUAD + e, 1)],
                                      ALU.mult).then_inc(bias_ready, 1)
                for e in range(QUAD):
                    dve.wait_ge(exp_ready, i * (2 * QUAD) + (2 * e + 2))
                    dve.reciprocal(SMALL[:, e, 3, :], SMALL[:, e, 2, :]).then_inc(den_ready, 1)
                    dve.wait_ge(den_ready, i * QUAD + (e + 1))
                    for b in range(TB):
                        dve.tensor_scalar(PN[:, e, b, :], PB[e][:, b, :], SMALL[:, e, 3, b:b + 1], None,
                                          ALU.mult).then_inc(probs_ready, 1)
                for e in range(QUAD):
                    dve.wait_ge(o_hi_ready, i * QUAD + (e + 1))
                    dve.tensor_tensor(H[:, ds(i * QUAD + (8 + e), 1), TOK:], PS[:, e, 0:TOK].unsqueeze(1),
                                      f32(H[:, ds(i * QUAD + (8 + e), 1), 0:TOK]), ALU.subtract).then_inc(o_lo_ready, 1)

            def conv_norm():
                inverse(ST_CONV, RINV2[:])
                dve.wait_ge(rinv_ready, ST_CONV + 1)
                dve.wait_ge(conv_pool, CONV_POOL_END)
                for t in (0, 4):
                    dve.tensor_tensor(Y[:, t:t + 4, :], Y[:, t:t + 4, :], over(RINV2[:], 4), ALU.mult).then_inc(y_scaled, 1)

            def swish_lo():
                for i, t in enumerate((0, 4)):
                    dve.wait_ge(a_hi_ready, i + 1)
                    dve.tensor_tensor(H[:, t:t + 4, TOK:], Y[:, t:t + 4, :], f32(H[:, t:t + 4, 0:TOK]),
                                      ALU.subtract).then_inc(a_lo_ready, 1)

            jobs = []
            for m in range(8):
                n, g = WO_N + 2 * m, WO_G + m
                for u in range(2):
                    if m:
                        split(n + u, u)
                    if jobs:
                        jobs.pop(0)()
                jobs = [lambda m=m, g=g: residual_add(g, m % 4, 1.0), lambda: None]
                if m == CONV_STAT_M:
                    jobs[0] = lambda m=m, g=g: (conv_norm(), residual_add(g, m, 1.0))
                if m == CONV_STAT_M + 1:
                    jobs[0] = lambda m=m, g=g: (swish_lo(), residual_add(g, m, 1.0))
                if m >= 4:
                    jobs[1] = lambda m=m: residual_lo(m - 4, "ffn2_norm", 4 + m)
            jobs = ffn(1, jobs, ST_FFN2)
            jobs[0]()
            inverse(ST_OUT, RINV[:])
            dve.wait_ge(rinv_ready, ST_OUT + 1)
            for m in range(4):
                dve.wait_ge(y_gained, 4 * m + 4)
                dve.tensor_tensor(YG[:, 4 * m:4 * m + 4, :], YG[:, 4 * m:4 * m + 4, :], over(RINV[:], 4),
                                  ALU.mult).then_inc(y_scaled_out, 1)

        @block.tensor
        def _(pe):
            mm = pe.matmul

            def unit(n, c, banks, width, ks, rhs, k_first, k_last, widths=None):
                s, second = c % 2, (len(ks) + 1) // 2
                for j, k in enumerate(ks):
                    if j in (0, second):
                        pe.wait_ge(wlo_ready, n * 2 + (1 if j == 0 else 2))
                    for t, bank in enumerate(banks):
                        w = P if widths is None else widths[t]
                        at = j * width + t * P
                        first, last = k == k_first, k == k_last

                        def hi():
                            return mm(PS[0:w, bank, :], WHI[:, s, at:at + w], rhs(k), start=first, stop=last)

                        def lo():
                            return mm(PS[0:w, bank, 0:TOK], WLO[:, s, at:at + w], rhs(k)[:, 0:TOK],
                                      start=False, stop=False)

                        if last:
                            lo()
                            ins = hi()
                        else:
                            hi()
                            ins = lo()
                    if j in (second - 1, len(ks) - 1):
                        ins.then_inc(units_used, 1)

            def xn(k):
                return XN[:, k, :]

            def hid(k):
                return H[:, k, :]

            def free(g):
                if not (isinstance(g, int) and g < 2):
                    pe.wait_ge(banks_free, g - 1)

            def bank_set(s, n=4):
                return list(range(4 * s, 4 * s + n))

            def stat(st, bank):
                pe.wait_ge(sq_added, SQ_END[st])
                mm(PS[:, bank, 0:TOK], ONES[:], SQ[:, 0, :], start=True, stop=False)
                mm(PS[:, bank, 0:TOK], ONES[:], SQ[:, 1, :], start=False, stop=True).then_inc(stat_done, 1)

            def latent_stat(st, bank, tiles):
                pe.wait_ge(latent_sq, 1 + (st == ST_ZQ))
                for t in range(tiles):
                    ins = mm(PS[:, bank, 0:TOK], ONES[:], SQB[:, t, :], start=(t == 0), stop=(t == tiles - 1))
                ins.then_inc(stat_done, 1)

            def pair(n, g, s, w=2, first=0, hook=None, residual=None):
                free(g)
                for c in range(KC):
                    if residual is not None:
                        pe.wait_ge(x_lo_ready, residual + 4 * (c + 1))
                    if c == 3 and hook:
                        hook()
                    unit(n + c, c, bank_set(s, 2 * w), 2 * w * P, range(KC * c, KC * c + KC), xn, 0, DT - 1)

            def ffn(f, hook, residual):
                for p, (_, nt) in enumerate(PARTS):
                    n, g, q0, _ = part_start(f, p)
                    s0 = g % 2
                    pair(n, g, s0, hook=hook if p == 0 else None, residual=residual if p == 0 else None)
                    if p == 0:
                        pe.wait_ge(root_ready, (ST_FFN1, ST_FFN2)[f] + 1)
                    pair(n + KC, g + 1, 1 - s0)
                    with pe.Fori(1, FULL_PAIRS[p] // 2) as i:
                        for e in range(2):
                            pair(i * (2 * KC) + (n + KC * e), i * 2 + (g + e), (s0 + e) % 2)
                    for q in range(FULL_PAIRS[p] // 2 * 2, PAIR_COUNT[p]):
                        pair(n + KC * q, g + q, (s0 + q) % 2, min(2, nt - 2 * q))
                    n, g, du = n + KC * PAIR_COUNT[p], g + PAIR_COUNT[p], DOWN_UNITS[p]

                    def down(n, g, s, c0):
                        free(g)
                        for u in range(du):
                            ks = range(KC * u, min(KC * u + KC, nt))
                            pe.wait_ge(h_lo_ready, q0 + (ks[-1] + 2) // 2)
                            unit(n + u, c0 + u, bank_set(s), 4 * P, ks, hid, 0, nt - 1)

                    with pe.Fori(0, 2) as i:
                        for e in range(2):
                            down(i * (2 * du) + (n + du * e), i * 2 + (g + e), (g + e) % 2, du * e)

            def ffn1_stat():
                pe.wait_ge(ones_ready, 1)
                stat(ST_FFN1, STAT_BANK[0])

            ffn(0, ffn1_stat, 0)

            def mix_stat():
                pe.wait_ge(banks_free, MIX_G)
                stat(ST_MIX, 4)

            pair(MIX_N, MIX_G, 0, hook=mix_stat, residual=16)
            pe.wait_ge(root_ready, ST_MIX + 1)
            for j in range(1, GLU_PAIRS):
                pair(MIX_N + KC * j, MIX_G + j, j % 2)
            free(KV_G)
            for c in range(KC):
                unit(MIX_N + 16 + c, c, [0, 1, 2], KVR + ROPE, range(KC * c, KC * c + KC), xn, 0, DT - 1, [P, P, ROPE])
            free(ZQ_G)
            for c in range(KC):
                if c == 3:
                    latent_stat(ST_KV, 0, KVR // P)
                unit(MIX_N + 20 + c, c, bank_set(1), 4 * P, range(KC * c, KC * c + KC), xn, 0, DT - 1)
            pe.wait_ge(root_ready, ST_KV + 1)
            pe.wait_ge(kv_lo, KVR // P)
            for h in range(2):
                pe.wait_ge(wlo_ready, 2 * (MIX_N + 25 + h))
                for b in range(TB):
                    for k in range(KVR // P):
                        hi, lo = H[:, 16 + k, b * P:(b + 1) * P], H[:, 16 + k, TOK + b * P:TOK + (b + 1) * P]
                        whi, wlo = WHI[:, h, 512 * k:512 * k + 512], WLO[:, h, 512 * k:512 * k + 512]
                        out = PS[:, 2 * b + h, :]
                        mm(out, hi, whi, start=(k == 0), stop=False)
                        mm(out, hi, wlo, start=False, stop=False)
                        ins = mm(out, lo, whi, start=False, stop=(k == 1))
                ins.then_inc(units_used, 2)
            latent_stat(ST_ZQ, 4, QR // P)
            pe.wait_ge(root_ready, ST_ZQ + 1)
            for h in range(2):
                free(K_G + h)
                unit(MIX_N + 26 + h, h, bank_set(1 - h), 512, range(2), lambda k: H[:, 16 + k, :], 0, 1)
            pe.wait_ge(zq_lo, QR // P)
            for h in range(2):
                free(R_G + h)
                unit(MIX_N + 28 + h, h, bank_set(1 - h, 2), 256, range(KC), xn, 0, KC - 1)
            pe.wait_ge(consts_loaded, 32)
            pe.wait_ge(kpe_sq, 1)
            for i in range(2):
                pe.wait_ge(hsq_ready, i + 1)
                for t in range(4):
                    ins = mm(PS[0:HEADS, 2, 0:TOK], SEL[:, 4 * i + t, :], (SQB, SUM[:])[i][:, t, :], start=(i + t == 0), stop=False)
                if i:
                    ins = mm(PS[0:HEADS, 2, 0:TOK], ONES[0:ROPE, 0:HEADS], KPSQ[:], start=False, stop=True)
                ins.then_inc(hstat_done, 1)
            for h in range(2):
                free(Q_G + h)
                if h:
                    pe.wait_ge(kroot_ready, 1)
                unit(MIX_N + 30 + h, h, bank_set(1 - h), 512, range(KC), xn, 0, KC - 1)

            def query_stat(i):
                pe.wait_ge(hsq_ready, i + 1)
                for t in range(4):
                    for b in range(TB):
                        if i > 2:
                            at, rhs = 4 * (i - 3) + t + 8 * b, ONES[:, 0:1]
                        else:
                            at, rhs = 16 + 2 * t + 8 * b, HALVES
                        ins = mm(PS[:, 7, at:at + rhs.shape[1]], (SQB, SUM[:])[i % 2][:, t, b * P:(b + 1) * P], rhs,
                                 start=True, stop=True)
                ins.then_inc(hstat_done, 1)

            pe.wait_ge(banks_free, Q_G + 1)
            query_stat(2)
            query_stat(3)
            pe.wait_ge(expand_loaded, 16)
            pe.wait_ge(krinv_ready, 1)
            for j in range(HEADS // 2):
                if j == HEADS // 2 - 1:
                    pe.wait_ge(banks_free, Q_G + 2)
                for e in range(2):
                    h = 2 * j + e
                    ins = mm(PS[:, KBCAST_BANKS[j], e * TOK:(e + 1) * TOK], EXPAND[:, h * P:(h + 1) * P], KRINV,
                             start=True, stop=True)
                ins.then_inc(kbcast_done if j < HEADS // 2 - 1 else o_done, 1)
            query_stat(4)
            pe.wait_ge(k_scaled, HEADS)
            pe.wait_ge(qrot_ready, 1)
            pe.wait_ge(qr_zeroed, 1)
            pe.wait_ge(o_lo_ready, 1)
            pe.wait_ge(ident_loaded, 16)
            with pe.Fori(0, HEADS // QUAD) as i:
                pe.wait_ge(o_lo_ready, i * QUAD + 1)
                for e in range(QUAD):
                    pe.wait_ge(q_static, i * QUAD + (e + 1))
                    pe.wait_ge(qr_static, i * QUAD + (e + 1))
                    for b in range(TB):
                        out = PS[:, e, b * TOK:(b + 1) * TOK]
                        mm(out, QS[:, e, b * P:(b + 1) * P],
                           KN[:, ds(i * QUAD + e, 1), :], start=True, stop=False)
                        ins = mm(out, QRS[:, e, b * P:(b + 1) * P], KRH[:, ds(i * 2 + e // 2, 1), :],
                                 start=False, stop=True)
                    ins.then_inc(scores_done, 1)
                for e in range(QUAD):
                    pe.wait_ge(probs_ready, i * (2 * QUAD) + (2 * e + 2))
                    for b in range(TB):
                        for k in range(TB):
                            ins = pe.transpose(PS[:, 4 + e, k * TOK + b * P:k * TOK + (b + 1) * P],
                                               PN[:, e, b, k * P:(k + 1) * P], IDENT[:])
                    ins.then_inc(probs_turned, 1)
                for e in range(QUAD):
                    pe.wait_ge(probsT_ready, i * QUAD + (e + 1))
                    pe.wait_ge(v_static, i * QUAD + (e + 1))
                    for k in range(TB):
                        ins = mm(PS[:, e, 0:TOK], VS[:, e, k, :], PT[:, e, k, :], start=(k == 0), stop=(k == 1))
                    ins.then_inc(o_done, 1)

            pe.wait_ge(o_lo_ready, HEADS + 1)
            for m in range(8):
                g, k0 = WO_G + m, CT if m < 4 else 0
                free(g)
                if m == CONV_STAT_M + 1:
                    pe.wait_ge(root_ready, ST_CONV + 1)
                for u in range(2):
                    if m == CONV_STAT_M and u == 1:
                        pe.wait_ge(banks_free, g)
                        stat(ST_CONV, CONV_STAT_BANK)
                    if m == 4:
                        pe.wait_ge(a_lo_ready, u + 1)
                    k = k0 + KC * u
                    unit(WO_N + 2 * m + u, u, bank_set(g % 2), 4 * P, range(k, k + KC), hid, k0, k0 + 2 * KC - 1)

            def ffn2_stat():
                pe.wait_ge(banks_free, FFN_G[1])
                stat(ST_FFN2, STAT_BANK[1])

            ffn(1, ffn2_stat, 32)
            pe.wait_ge(banks_free, FFN_G[1] + FFN_GROUPS - 1)
            stat(ST_OUT, OUT_BANK)


def kernel(**inputs):
    import concourse.bacc as bacc
    from concourse.bass_utils import run_bass_kernel_spmd

    nc = bacc.Bacc("TRN2", target_bir_lowering=False, num_devices=1)
    lane = np.arange(P)
    freq = (10000.0 ** (-(np.arange(ROPE // 2, dtype=np.float32) * 2.0 / ROPE))).astype(np.float32)
    consts = {
        "ident": np.eye(P, dtype=np.float32),
        "sel": np.ascontiguousarray(np.broadcast_to(np.eye(HEADS, dtype=np.float32), (P, HEADS, HEADS))),
        "expand": np.repeat(np.eye(HEADS, dtype=np.float32), P, axis=1),
        "freq": np.stack([freq[lane % 32], np.where(lane % 64 < 32, -1.0, 1.0), lane < ROPE, lane >= ROPE], 1).astype(np.float32),
    }
    def tiles(a):
        return a.reshape(-1, P, *a.shape[1:]).swapaxes(0, 1)

    laid = {k: inputs[k] for k in WEIGHTS}
    laid["positions"] = inputs["positions"]
    laid["x"] = tiles(inputs["x"][0].T)
    laid["taps"] = tiles(inputs["dw_kernel"][0].T).reshape(P, CT * TAPS)
    q, k = inputs["q_head_norm"][0], inputs["k_head_norm"][0]
    heads = [q[:NOPE], k[:NOPE], np.tile(q[NOPE:], 2), np.tile(k[NOPE:], 2)]
    laid["gains"] = np.concatenate([tiles(inputs[n][0]) for n, _ in GAIN_ROWS] + [np.stack(heads, 1)], 1)
    arrays, io = {}, {}
    for name, a in {**laid, **consts}.items():
        a = np.ascontiguousarray(a)
        arrays[f"in_{name}"] = a
        io[name] = nc.dram_tensor(f"in_{name}", a.shape, mybir.dt.from_np(a.dtype), kind="ExternalInput").ap()
    io["y"] = nc.dram_tensor("out_y", (P, DT, TOK), F32, kind="ExternalOutput").ap()
    build_layer(nc, io)
    y = run_bass_kernel_spmd(nc, [arrays], core_ids=[0]).results[0]["out_y"]
    return np.ascontiguousarray(y.transpose(2, 1, 0).reshape(1, TOK, DM))
```
